# Optimizing a Trainium2 kernel written in Bass

```python
import math
import jax
import jax.numpy as jnp
from jax import lax
import numpy as np

D_MODEL = 1024
BATCH = 1
SEQ = 128
DEPTH = 2
DEC_BATCH = 1
DEC_SEQ = 256
PAST_LEN = 128

GRID_W = 64
N_MIXERS = 2
N_SSD_LAYERS = (DEPTH + 1) // 2
N_GDN_LAYERS = DEPTH // 2

SSD_D_INNER = 2 * D_MODEL
SSD_HEADDIM = 64
SSD_HEADS = SSD_D_INNER // SSD_HEADDIM
SSD_GROUPS = 8
SSD_STATE = 128
SSD_CONV = 3
SSD_CHUNK = 128
SSD_XBC = SSD_D_INNER + 2 * SSD_GROUPS * SSD_STATE
SSD_IN = SSD_D_INNER + SSD_XBC + 2 * SSD_HEADS

GDN_K_HEADS = 8
GDN_V_HEADS = 16
GDN_HEAD_K = 128
GDN_HEAD_V = 128
GDN_QK = GDN_K_HEADS * GDN_HEAD_K
GDN_V = GDN_V_HEADS * GDN_HEAD_V
GDN_QKV = 2 * GDN_QK + GDN_V
GDN_CONV = 3
GDN_CHUNK = 64
GDN_IN = GDN_QKV + GDN_V + 4 * GDN_V_HEADS

D_FF = 2816
FFN_CONV = 3

DEEPNORM_ALPHA = (2.0 * DEPTH) ** 0.25
DEEPNORM_BETA = (8.0 * DEPTH) ** -0.25
LN_EPS = 1e-5
RMS_EPS = 1e-6

kernel_name = 'bidir_ssd_gdn_prefix_dit_step'

def layer_norm(x, g, b):
    xf = x.astype(jnp.float32)
    mu = jnp.mean(xf, axis=-1, keepdims=True)
    var = jnp.mean(jnp.square(xf - mu), axis=-1, keepdims=True)
    return ((xf - mu) * lax.rsqrt(var + LN_EPS)).astype(x.dtype) * g + b

def rms_norm(x, w):
    xf = x.astype(jnp.float32)
    ms = jnp.mean(jnp.square(xf), axis=-1, keepdims=True)
    return (xf * lax.rsqrt(ms + RMS_EPS)).astype(x.dtype) * w

def l2_normalize(x):
    xf = x.astype(jnp.float32)
    return (xf * lax.rsqrt(jnp.sum(jnp.square(xf), axis=-1, keepdims=True) + RMS_EPS)).astype(x.dtype)

def adaln_params(cond, w_ada, b_ada):
    ada = (jax.nn.silu(cond) @ w_ada + b_ada)[:, None, :]
    return tuple(jnp.split(ada, 6, axis=-1))

def modulate(x, shift, scale):
    return x * (1.0 + scale) + shift

def dwconv1d_centred(x, w):
    width = w.shape[0]
    pad = width // 2
    seqlen = x.shape[1]
    xp = jnp.pad(x, ((0, 0), (pad, pad), (0, 0)))
    return sum(w[t] * xp[:, t:t + seqlen] for t in range(width))

def dwconv2d_grid(x, w, rows):
    bsz, seqlen, ch = x.shape
    img = x.reshape(bsz, rows, GRID_W, ch)
    out = lax.conv_general_dilated(img, w[:, :, None, :], window_strides=(1, 1), padding='SAME',
                                   dimension_numbers=('NHWC', 'HWIO', 'NHWC'), feature_group_count=ch)
    return out.reshape(bsz, seqlen, ch)

def flip_seq(t):
    return jnp.flip(t, axis=1)

def ssd_scan(x, dt, a_neg, b_mat, c_mat, s0):
    bsz, seqlen, nh, hp = x.shape
    ng, ns = b_mat.shape[2], b_mat.shape[3]
    nr = nh // ng
    nc = seqlen // SSD_CHUNK
    xc = x.reshape(bsz, nc, SSD_CHUNK, ng, nr, hp)
    dtc = dt.reshape(bsz, nc, SSD_CHUNK, ng, nr)
    bc = b_mat.reshape(bsz, nc, SSD_CHUNK, ng, ns)
    cc = c_mat.reshape(bsz, nc, SSD_CHUNK, ng, ns)
    acum = jnp.cumsum(dtc * a_neg.reshape(ng, nr), axis=2)
    xdt = xc * dtc[..., None]
    seg = acum[:, :, :, None] - acum[:, :, None, :]
    mask = jnp.tril(jnp.ones((SSD_CHUNK, SSD_CHUNK), dtype=bool))[:, :, None, None]
    decay = jnp.exp(jnp.where(mask, seg, -jnp.inf))
    scores = jnp.einsum('bcign,bcjgn->bcijg', cc, bc)
    y_intra = jnp.einsum('bcijgr,bcjgrp->bcigrp', scores[..., None] * decay, xdt)
    decay_end = jnp.exp(acum[:, :, -1:] - acum)
    states = jnp.einsum('bcqgn,bcqgr,bcqgrp->bcgrpn', bc, decay_end, xdt)
    chunk_decay = jnp.exp(acum[:, :, -1])

    def step(s, inp):
        st, dc = inp
        s_new = dc[..., None, None] * s + st
        return s_new.astype(s.dtype), s

    s_init = s0.reshape(bsz, ng, nr, hp, ns).astype(x.dtype)
    s_final, s_prev = lax.scan(step, s_init, (jnp.moveaxis(states, 1, 0), jnp.moveaxis(chunk_decay, 1, 0)))
    s_prev = jnp.moveaxis(s_prev, 0, 1)
    y_inter = jnp.einsum('bcign,bcgrpn,bcigr->bcigrp', cc, s_prev, jnp.exp(acum))
    y = (y_intra + y_inter).reshape(bsz, seqlen, nh, hp)
    return y, s_final.reshape(bsz, nh, hp, ns)

def gdn_scan(q, k, v, g, beta, s0):
    bsz, seqlen, nh, dk = q.shape
    dv = v.shape[-1]
    nc = seqlen // GDN_CHUNK

    def chunks(t):
        return jnp.moveaxis(t.reshape(bsz, nc, GDN_CHUNK, nh, -1), 3, 2)

    qc, kc, vc = chunks(q), chunks(k), chunks(v)
    gc = jnp.cumsum(jnp.moveaxis(g.reshape(bsz, nc, GDN_CHUNK, nh), 3, 2), axis=-1)
    bc = jnp.moveaxis(beta.reshape(bsz, nc, GDN_CHUNK, nh), 3, 2)[..., None]
    seg = gc[..., :, None] - gc[..., None, :]
    incl = jnp.tril(jnp.ones((GDN_CHUNK, GDN_CHUNK), dtype=bool))
    strict = jnp.tril(jnp.ones((GDN_CHUNK, GDN_CHUNK), dtype=bool), -1)
    kb = kc * bc
    a_mat = jnp.einsum('bchid,bchjd->bchij', kb, kc) * jnp.exp(jnp.where(strict, seg, -jnp.inf))
    sys_mat = (jnp.eye(GDN_CHUNK, dtype=jnp.float32) + a_mat.astype(jnp.float32))
    rhs = jnp.concatenate([vc * bc, kb * jnp.exp(gc)[..., None]], axis=-1).astype(jnp.float32)
    sol = lax.linalg.triangular_solve(sys_mat, rhs, left_side=True, lower=True, unit_diagonal=True).astype(q.dtype)
    u, w = sol[..., :dv], sol[..., dv:]
    qk = jnp.einsum('bchid,bchjd->bchij', qc, kc) * jnp.exp(jnp.where(incl, seg, -jnp.inf))
    q_dec = qc * jnp.exp(gc)[..., None]
    k_dec = kc * jnp.exp(gc[..., -1:] - gc)[..., None]
    g_last = jnp.exp(gc[..., -1])

    def step(s, inp):
        u_c, w_c, qk_c, qd_c, kd_c, gl_c = inp
        v_new = u_c - jnp.einsum('bhid,bhde->bhie', w_c, s)
        o_c = jnp.einsum('bhid,bhde->bhie', qd_c, s) + jnp.einsum('bhij,bhje->bhie', qk_c, v_new)
        s_new = gl_c[..., None, None] * s + jnp.einsum('bhjd,bhje->bhde', kd_c, v_new)
        return s_new.astype(s.dtype), o_c

    xs = tuple(jnp.moveaxis(t, 1, 0) for t in (u, w, qk, q_dec, k_dec, g_last))
    s_final, o = lax.scan(step, s0.astype(q.dtype), xs)
    o = jnp.moveaxis(jnp.moveaxis(o, 0, 1), 2, 3).reshape(bsz, seqlen, nh, dv)
    return o, s_final

def ssd_mixer(h, s0_f, s0_b, w_in, conv_w, conv_b, dt_bias, a_log, d_skip, norm_w, w_out):
    bsz, seqlen, _ = h.shape
    proj = h @ w_in
    z = proj[..., :SSD_D_INNER]
    xbc = jax.nn.silu(dwconv1d_centred(proj[..., SSD_D_INNER:SSD_D_INNER + SSD_XBC], conv_w) + conv_b)
    dt_raw = proj[..., SSD_D_INNER + SSD_XBC:].reshape(bsz, seqlen, 2, SSD_HEADS)
    xs = xbc[..., :SSD_D_INNER].reshape(bsz, seqlen, SSD_HEADS, SSD_HEADDIM)
    gn = SSD_GROUPS * SSD_STATE
    bm = xbc[..., SSD_D_INNER:SSD_D_INNER + gn].reshape(bsz, seqlen, SSD_GROUPS, SSD_STATE)
    cm = xbc[..., SSD_D_INNER + gn:].reshape(bsz, seqlen, SSD_GROUPS, SSD_STATE)
    dt = jax.nn.softplus(dt_raw + dt_bias)
    a_neg = -jnp.exp(a_log)
    y_f, s_f = ssd_scan(xs, dt[:, :, 0], a_neg[0], bm, cm, s0_f)
    y_b, s_b = ssd_scan(flip_seq(xs), flip_seq(dt[:, :, 1]), a_neg[1], flip_seq(bm), flip_seq(cm), s0_b)
    y = y_f + flip_seq(y_b) + xs * d_skip[:, None]
    y = rms_norm(y.reshape(bsz, seqlen, SSD_D_INNER) * jax.nn.silu(z), norm_w)
    return y @ w_out, s_f, s_b

def gdn_mixer(h, s0_f, s0_b, w_in, conv_w, dt_bias, a_log, norm_w, w_out):
    bsz, seqlen, _ = h.shape
    proj = h @ w_in
    qkv = jax.nn.silu(dwconv1d_centred(proj[..., :GDN_QKV], conv_w))
    q = qkv[..., :GDN_QK].reshape(bsz, seqlen, GDN_K_HEADS, GDN_HEAD_K)
    k = qkv[..., GDN_QK:2 * GDN_QK].reshape(bsz, seqlen, GDN_K_HEADS, GDN_HEAD_K)
    v = qkv[..., 2 * GDN_QK:].reshape(bsz, seqlen, GDN_V_HEADS, GDN_HEAD_V)
    z = proj[..., GDN_QKV:GDN_QKV + GDN_V].reshape(bsz, seqlen, GDN_V_HEADS, GDN_HEAD_V)
    a_raw = proj[..., GDN_QKV + GDN_V:GDN_QKV + GDN_V + 2 * GDN_V_HEADS].reshape(bsz, seqlen, 2, GDN_V_HEADS)
    b_raw = proj[..., GDN_QKV + GDN_V + 2 * GDN_V_HEADS:].reshape(bsz, seqlen, 2, GDN_V_HEADS)
    rep = GDN_V_HEADS // GDN_K_HEADS
    q = jnp.repeat(l2_normalize(q) * (GDN_HEAD_K ** -0.5), rep, axis=2)
    k = jnp.repeat(l2_normalize(k), rep, axis=2)
    g = -jnp.exp(a_log) * jax.nn.softplus(a_raw + dt_bias)
    beta = jax.nn.sigmoid(b_raw)
    o_f, s_f = gdn_scan(q, k, v, g[:, :, 0], beta[:, :, 0], s0_f)
    o_b, s_b = gdn_scan(flip_seq(q), flip_seq(k), flip_seq(v), flip_seq(g[:, :, 1]), flip_seq(beta[:, :, 1]), s0_b)
    o = rms_norm(o_f + flip_seq(o_b), norm_w) * jax.nn.silu(z)
    return o.reshape(bsz, seqlen, GDN_V) @ w_out, s_f, s_b

def conv_glu_ffn(h, w_up, conv_w, conv_b, w_down, rows):
    up = h @ w_up
    a, v = up[..., :D_FF], up[..., D_FF:]
    if rows is None:
        a = dwconv1d_centred(a, conv_w[FFN_CONV // 2])
    else:
        a = dwconv2d_grid(a, conv_w, rows)
    return (jax.nn.silu(a + conv_b) * v) @ w_down

def _dt_bias_init(k, shape):
    dt = jnp.exp(jax.random.uniform(k, shape, jnp.float32, math.log(1e-3), math.log(1e-1)))
    return dt + jnp.log(-jnp.expm1(-dt))

def setup_inputs(seed: int = 0) -> dict:
    key = jax.random.key(seed)
    ks = jax.random.split(key, 32)

    def nrm(k, shape, scale):
        return jax.random.normal(k, shape, jnp.float32) * scale

    return {
        'x_prompt': nrm(ks[0], (BATCH, SEQ, D_MODEL), 1.0),
        'x_sample': nrm(ks[1], (DEC_BATCH, DEC_SEQ, D_MODEL), 1.0),
        'state_ssd_fwd': nrm(ks[2], (DEC_BATCH, N_SSD_LAYERS, SSD_HEADS, SSD_HEADDIM, SSD_STATE), 0.1),
        'state_ssd_bwd': nrm(ks[3], (DEC_BATCH, N_SSD_LAYERS, SSD_HEADS, SSD_HEADDIM, SSD_STATE), 0.1),
        'state_gdn_fwd': nrm(ks[4], (DEC_BATCH, N_GDN_LAYERS, GDN_V_HEADS, GDN_HEAD_K, GDN_HEAD_V), 0.1),
        'state_gdn_bwd': nrm(ks[5], (DEC_BATCH, N_GDN_LAYERS, GDN_V_HEADS, GDN_HEAD_K, GDN_HEAD_V), 0.1),
        'c': nrm(ks[6], (DEC_BATCH, D_MODEL), 1.0),
        'c_ctx': nrm(ks[7], (D_MODEL,), 1.0),
        'w_ada': nrm(ks[8], (DEPTH, D_MODEL, 6 * D_MODEL), D_MODEL ** -0.5),
        'b_ada': nrm(ks[9], (DEPTH, 6 * D_MODEL), 0.02),
        'ln_g': 1.0 + nrm(ks[10], (DEPTH, 2, D_MODEL), 0.01),
        'ln_b': nrm(ks[11], (DEPTH, 2, D_MODEL), 0.01),
        'ssd_w_in': nrm(ks[12], (N_SSD_LAYERS, D_MODEL, SSD_IN), D_MODEL ** -0.5),
        'ssd_conv_w': nrm(ks[13], (N_SSD_LAYERS, SSD_CONV, SSD_XBC), SSD_CONV ** -0.5),
        'ssd_conv_b': nrm(ks[14], (N_SSD_LAYERS, SSD_XBC), 0.02),
        'ssd_dt_bias': _dt_bias_init(ks[15], (N_SSD_LAYERS, 2, SSD_HEADS)),
        'ssd_a_log': jnp.log(jax.random.uniform(ks[16], (N_SSD_LAYERS, 2, SSD_HEADS), jnp.float32, 1.0, 16.0)),
        'ssd_d': 1.0 + nrm(ks[17], (N_SSD_LAYERS, SSD_HEADS), 0.1),
        'ssd_norm_w': 1.0 + nrm(ks[18], (N_SSD_LAYERS, SSD_D_INNER), 0.01),
        'ssd_w_out': nrm(ks[19], (N_SSD_LAYERS, SSD_D_INNER, D_MODEL), SSD_D_INNER ** -0.5 * DEEPNORM_BETA),
        'gdn_w_in': nrm(ks[20], (N_GDN_LAYERS, D_MODEL, GDN_IN), D_MODEL ** -0.5),
        'gdn_conv_w': nrm(ks[21], (N_GDN_LAYERS, GDN_CONV, GDN_QKV), GDN_CONV ** -0.5),
        'gdn_dt_bias': _dt_bias_init(ks[22], (N_GDN_LAYERS, 2, GDN_V_HEADS)),
        'gdn_a_log': jnp.log(jax.random.uniform(ks[23], (N_GDN_LAYERS, 2, GDN_V_HEADS), jnp.float32, 1.0, 16.0)),
        'gdn_norm_w': 1.0 + nrm(ks[24], (N_GDN_LAYERS, GDN_HEAD_V), 0.01),
        'gdn_w_out': nrm(ks[25], (N_GDN_LAYERS, GDN_V, D_MODEL), GDN_V ** -0.5 * DEEPNORM_BETA),
        'ffn_w_up': nrm(ks[26], (DEPTH, D_MODEL, 2 * D_FF), D_MODEL ** -0.5),
        'ffn_conv_w': nrm(ks[27], (DEPTH, FFN_CONV, FFN_CONV, D_FF), 1.0 / FFN_CONV),
        'ffn_conv_b': nrm(ks[28], (DEPTH, D_FF), 0.02),
        'ffn_w_down': nrm(ks[29], (DEPTH, D_FF, D_MODEL), D_FF ** -0.5 * DEEPNORM_BETA),
    }

def reference(x_prompt, x_sample, state_ssd_fwd, state_ssd_bwd, state_gdn_fwd, state_gdn_bwd, c, c_ctx,
              w_ada, b_ada, ln_g, ln_b,
              ssd_w_in, ssd_conv_w, ssd_conv_b, ssd_dt_bias, ssd_a_log, ssd_d, ssd_norm_w, ssd_w_out,
              gdn_w_in, gdn_conv_w, gdn_dt_bias, gdn_a_log, gdn_norm_w, gdn_w_out,
              ffn_w_up, ffn_conv_w, ffn_conv_b, ffn_w_down):
    rows = x_sample.shape[1] // GRID_W
    n_prompt = x_prompt.shape[0]
    xp, xs = x_prompt, x_sample
    cond_ctx = c_ctx[None, :]
    new_ssd_f, new_ssd_b, new_gdn_f, new_gdn_b = [], [], [], []
    for i in range(DEPTH):
        sh_mp, sc_mp, gt_mp, sh_fp, sc_fp, gt_fp = adaln_params(cond_ctx, w_ada[i], b_ada[i])
        sh_ms, sc_ms, gt_ms, sh_fs, sc_fs, gt_fs = adaln_params(c, w_ada[i], b_ada[i])
        hp = modulate(xp, sh_mp, sc_mp)
        hs = modulate(xs, sh_ms, sc_ms)
        j = i // N_MIXERS
        if i % N_MIXERS == 0:
            prm = (ssd_w_in[j], ssd_conv_w[j], ssd_conv_b[j], ssd_dt_bias[j], ssd_a_log[j], ssd_d[j],
                   ssd_norm_w[j], ssd_w_out[j])
            zeros = jnp.zeros((n_prompt, SSD_HEADS, SSD_HEADDIM, SSD_STATE), xp.dtype)
            mp, sf, sb = ssd_mixer(hp, zeros, zeros, *prm)
            ms, _, _ = ssd_mixer(hs, state_ssd_fwd[:, j], state_ssd_bwd[:, j], *prm)
            new_ssd_f.append(sf)
            new_ssd_b.append(sb)
        else:
            prm = (gdn_w_in[j], gdn_conv_w[j], gdn_dt_bias[j], gdn_a_log[j], gdn_norm_w[j], gdn_w_out[j])
            zeros = jnp.zeros((n_prompt, GDN_V_HEADS, GDN_HEAD_K, GDN_HEAD_V), xp.dtype)
            mp, sf, sb = gdn_mixer(hp, zeros, zeros, *prm)
            ms, _, _ = gdn_mixer(hs, state_gdn_fwd[:, j], state_gdn_bwd[:, j], *prm)
            new_gdn_f.append(sf)
            new_gdn_b.append(sb)
        xp = layer_norm(DEEPNORM_ALPHA * xp + gt_mp * mp, ln_g[i, 0], ln_b[i, 0])
        xs = layer_norm(DEEPNORM_ALPHA * xs + gt_ms * ms, ln_g[i, 0], ln_b[i, 0])
        fp = conv_glu_ffn(modulate(xp, sh_fp, sc_fp), ffn_w_up[i], ffn_conv_w[i], ffn_conv_b[i], ffn_w_down[i], None)
        fs = conv_glu_ffn(modulate(xs, sh_fs, sc_fs), ffn_w_up[i], ffn_conv_w[i], ffn_conv_b[i], ffn_w_down[i], rows)
        xp = layer_norm(DEEPNORM_ALPHA * xp + gt_fp * fp, ln_g[i, 1], ln_b[i, 1])
        xs = layer_norm(DEEPNORM_ALPHA * xs + gt_fs * fs, ln_g[i, 1], ln_b[i, 1])
    y_prompt = xp
    y_sample = xs
    new_state_ssd_fwd = jnp.stack(new_ssd_f, axis=1)
    new_state_ssd_bwd = jnp.stack(new_ssd_b, axis=1)
    new_state_gdn_fwd = jnp.stack(new_gdn_f, axis=1)
    new_state_gdn_bwd = jnp.stack(new_gdn_b, axis=1)
    return (y_prompt, y_sample, new_state_ssd_fwd, new_state_ssd_bwd, new_state_gdn_fwd, new_state_gdn_bwd)


_drawn_inputs = setup_inputs


def setup_inputs(seed=0):
    import zlib

    import numpy as np

    out = dict(_drawn_inputs(seed))
    spreads = {}
    factors = {'state_ssd_fwd': 4.839,
     'state_ssd_bwd': 3.956,
     'state_gdn_fwd': 4.714,
     'state_gdn_bwd': 4.429,
     'ln_b': 2.766,
     'ssd_d': 8.0,
     'ssd_norm_w': 8.0,
     'gdn_norm_w': 8.0,
     'ffn_conv_b': 8.0}
    for name, (base, spread) in spreads.items():
        noise = np.random.default_rng([zlib.crc32(name.encode()), seed]).standard_normal(out[name].shape)
        drawn = base * np.exp(spread * noise) if base else spread * noise
        out[name] = jnp.asarray(drawn.astype(out[name].dtype))
    for name, factor in factors.items():
        out[name] = (out[name] * factor).astype(out[name].dtype)
    return out
```

```python
from contextlib import ExitStack

import concourse.bass as bass
from concourse import mybir

F32 = mybir.dt.float32
F32R = mybir.dt.float32r
BF16 = mybir.dt.bfloat16
ALU = mybir.AluOpType
ACT = mybir.ActivationFunctionType
AX_X = mybir.AxisListType.X

P = 128
DEPTH = 2
D = 1024
DT = D // P
TOK = 384
NCH = TOK // P
CTX, LAT1, LAT2 = range(NCH)
GRID_W = 64
GRID_H = 256 // GRID_W
N_IN = 49
CONV_T = 32
GATE_T = 16
N_OUT = 2 * DT
FF = 2816
FF_T = FF // P
N_DOWN = 2 * DT
KT_IN = DT
KT_DOWN = FF_T // 2
ALPHA = 4.0 ** 0.25
LN_EPS = 1e-5
RMS_EPS = 1e-6
SSD_H, SSD_P, SSD_G = 32, 64, 8
GDN_H, GDN_KH = 16, 8
LEVELS = 7
RAW = 4
SPL = 2

VEC = {}
_at = 0
for _name, _n in (("b_ada", 2 * 48), ("ln_g", 2 * 2 * DT), ("ln_b", 2 * 2 * DT), ("conv_w", 2 * CONV_T * 3),
                  ("conv_b", 2 * CONV_T), ("dt_bias", 2), ("a_log", 2), ("d_skip", 16), ("ssd_norm", 16),
                  ("gdn_norm", 1), ("ffn_w", 2 * FF_T * 9), ("ffn_b", 2 * FF_T), ("cond", DT * 2), ("eps", 4)):
    VEC[_name] = (_at, _at + _n)
    _at += _n
NVEC = _at
MASKS = ("ident", "le", "ge", "gt", "lt", "ones")


class Idx:

    def __init__(self, base, i=None, step=0):
        self.base, self.i, self.step = base, i, step

    def __mul__(self, n):
        return Idx(self.base * n, self.i, self.step * n)

    def __add__(self, n):
        return Idx(self.base + n, self.i, self.step)

    @property
    def val(self):
        return self.base if self.i is None else self.i * self.step + self.base

    def mod(self, m):
        assert self.i is None or self.step % m == 0
        return self.base % m

    def div(self, m):
        assert self.i is None or self.step % m == 0
        return Idx(self.base // m, self.i, self.step // m)


def steps(eng, lo, hi, body):
    n = (hi - lo) // 4
    if n > 1:
        with eng.Fori(0, n) as i:
            for k in range(4):
                body(Idx(lo + k, i, 4))
        lo += 4 * n
    for k in range(lo, hi):
        body(Idx(k))


class Phase:

    def __init__(self, name, kind, n, kt, src, raw0, own0):
        self.name, self.kind, self.n, self.kt, self.src = name, kind, n, kt, src
        self.raw0, self.own0 = raw0, own0





def trunk(nc, io):
    ctx = ExitStack()
    with ctx:
        def sem(name):
            return ctx.enter_context(nc.semaphore(name))

        top = [(nc.sbuf_base + 31) // 32 * 32]
        WORD = {F32: 4, F32R: 4, BF16: 2}

        def nbytes(shape, dt):
            n = WORD[dt]
            for x in shape[1:]:
                n *= x
            return (n + 31) // 32 * 32

        def put(name, shape, dt, at=None):
            where = top[0] if at is None else at
            if at is None:
                top[0] += nbytes(shape, dt)
                assert top[0] <= nc.sbuf_usable_end, (name, top[0])
            return nc.alloc_sbuf_tensor_at(name, list(shape), dt, offset=where)

        masks = put("masks", [P, len(MASKS), P], F32)
        level = put("level", [P, 2, LEVELS, P], BF16)
        vec = put("vec", [P, NVEC], F32)
        ada = put("ada", [P, 2, 48, 2], F32)
        raw = put("raw", [P, RAW, KT_DOWN * P], F32)
        xr = put("xr", [P, DT, TOK], F32)
        scond = put("scond", [P, DT, 2], F32)
        ea = put("ea", [P, 1], F32)
        small = put("small", [P, 3 * TOK], F32)
        ss = put("ss", [P, NCH, 3, 4], F32)
        scratch0 = top[0]
        whi = put("whi", [P, SPL, KT_DOWN * P], F32R)
        wlo = put("wlo", [P, SPL, KT_DOWN * P], F32R)
        hhi_at = top[0]
        hhi = put("hhi", [P, DT, TOK], F32R)
        hlo = put("hlo", [P, DT, TOK], F32R)
        top_evac = top[0]
        evac = put("evac", [P, 8, TOK], F32)
        work0 = top[0]
        proj0 = nc.sbuf_usable_end // 32 * 32 - nbytes([P, 48, TOK], F32)
        proj = put("proj", [P, 48, TOK], F32, at=proj0)
        conv_out = proj[:, 0:CONV_T, :]
        gate = proj[:, CONV_T:48, :]
        yhi = put("yhi", [P, 16, TOK], F32R, at=proj0)
        ylo = put("ylo", [P, 16, TOK], F32R, at=proj0 + nbytes([P, 16, TOK], F32))
        ghi = put("ghi", [P, FF_T, TOK], F32R, at=proj0)
        glo = put("glo", [P, FF_T, TOK], F32R, at=proj0 + nbytes([P, FF_T, TOK], F32))
        sq = put("sq", [P, DT, TOK], F32, at=proj0)
        hmod = put("hmod", [P, DT, TOK], F32, at=proj0 + nbytes([P, DT, TOK], F32))
        assert work0 <= proj0, (work0, proj0)

        def mask(name):
            return masks[:, MASKS.index(name), :]

        def v(name):
            a, b = VEC[name]
            return vec[:, a:b]

        eps = v("eps")
        ident, ones = mask("ident"), mask("ones")
        cond = v("cond").rearrange("p (k c) -> p k c", c=2)
        ps = ctx.enter_context(nc.psum_tensor("ps", [P, 8, 512], F32))

        order, raw_n, own_n = [], 0, {"ada": 0, "split": 0}
        for name, kind, n, kt, src in (
                ("ada0", "ada", 48, KT_IN, io["w_ada"][0]), ("ssd_in", "split", N_IN, KT_IN, io["w_in"][0]),
                ("ssd_out", "split", N_OUT, KT_IN, io["w_out"][0]),
                ("up0", "split", 2 * FF_T, KT_IN, io["w_up"][0]), ("down0", "split", N_DOWN, KT_DOWN, io["w_down"][0]),
                ("ada1", "ada", 48, KT_IN, io["w_ada"][1]), ("gdn_in", "split", N_IN, KT_IN, io["w_in"][1]),
                ("gdn_out", "split", N_OUT, KT_IN, io["w_out"][1]),
                ("up1", "split", 2 * FF_T, KT_IN, io["w_up"][1]), ("down1", "split", N_DOWN, KT_DOWN, io["w_down"][1])):
            order.append(Phase(name, kind, n, kt, src, raw_n, own_n[kind]))
            raw_n += n
            own_n[kind] += n
        order = order[:5 * DEPTH]
        phase = {p.name: p for p in order}

        consts_in, x_in = sem("consts_in"), sem("x_in")
        raw_in = [sem(f"raw_in{s}") for s in range(RAW)]
        ada_used = sem("ada_used")
        hi_ready = sem("hi_ready")
        lo_ready = sem("lo_ready")
        blk_done = sem("blk_done")
        cond_silu = sem("cond_silu")
        ada_mm = sem("ada_mm")
        ada_ready = sem("ada_ready")
        h_mod, h_hi, h_lo = sem("h_mod"), sem("h_hi"), sem("h_lo")
        centre = sem("centre")
        left = sem("left")
        conv_done = sem("conv_done")
        conv_silu = sem("conv_silu")
        gate_done = sem("gate_done")
        gated = sem("gated")
        resid = sem("resid")
        f_centre = sem("f_centre")
        f_tap = sem("f_tap")
        up_out = sem("up_out")
        f_silu = sem("f_silu")
        g_hi, g_lo = sem("g_hi"), sem("g_lo")
        ln_mm, ln_mean, ln_cent, ln_sq, ln_std, ln_rstd, ln_norm, ln_x = (
            sem(x) for x in ("ln_mm", "ln_mean", "ln_cent", "ln_sq", "ln_std", "ln_rstd", "ln_norm", "ln_x"))
        y_scaled, y_hi, y_lo = sem("y_scaled"), sem("y_hi"), sem("y_lo")
        rms_sq, rms_mm, rms_std, rms_rstd = sem("rms_sq"), sem("rms_mm"), sem("rms_std"), sem("rms_rstd")
        dt_abs, dt_exp, dt_one, dt_ln, dt_rows, dt_tr, dt_tok, dt_cum, dt_dec, dt_last, dt_ch = (
            sem(x) for x in ("dt_abs", "dt_exp", "dt_one", "dt_ln", "dt_rows", "dt_tr", "dt_tok", "dt_cum", "dt_dec",
                             "dt_last", "dt_ch"))
        out_done = sem("out_done")

        def used(b):
            for p in order:
                if p.raw0 <= b < p.raw0 + p.n:
                    return (ada_used if p.kind == "ada" else lo_ready), p.own0 + b - p.raw0

        def load_weights(sp, p):
            def one(j):
                b = j + p.raw0
                if j.base >= RAW:
                    sp.wait_ge(ada_used if p.kind == "ada" else lo_ready, (j + (p.own0 - RAW + 1)).val)
                elif b.base >= RAW:
                    s, count = used(b.base - RAW)
                    sp.wait_ge(s, count + 1)
                sp.dma_start(raw[:, b.mod(RAW), 0:p.kt * P], p.src[j.val]).then_inc(raw_in[b.mod(RAW)], 16)

            for k in range(RAW):
                one(Idx(k))
            steps(sp, RAW, p.n, one)

        def split_hi(act, p, j):
            b, s = j + p.raw0, j + p.own0
            act.wait_ge(raw_in[b.mod(RAW)], ((b.div(RAW) + 1) * 16).val)
            act.wait_ge(blk_done, (s + 1).val)
            act.activation(whi[:, s.mod(SPL), 0:p.kt * P], raw[:, b.mod(RAW), 0:p.kt * P], ACT.Copy).then_inc(hi_ready, 1)

        def split_lo(pool, p):
            def one(j):
                b, s = j + p.raw0, j + p.own0
                pool.wait_ge(hi_ready, (s + 1).val)
                pool.tensor_tensor(wlo[:, s.mod(SPL), 0:p.kt * P], raw[:, b.mod(RAW), 0:p.kt * P],
                                   whi[:, s.mod(SPL), 0:p.kt * P].bitcast(F32), ALU.subtract).then_inc(lo_ready, 1)
            steps(pool, 0, p.n, one)

        def multiply(pe, p, lo, hi, q, rhi, rlo, free, free0, banks):
            pe.sem_inc(free, banks)

            def one(j):
                s, t, half = j + p.own0, j.div(q), j.base % q
                pe.wait_ge(lo_ready, (s + 1).val)
                if half == 0:
                    pe.wait_ge(free, (t + (free0 + 1 - lo)).val)
                out = ps[:, t.mod(banks), 0:TOK]
                for k in range(p.kt):
                    a = whi[:, s.mod(SPL), k * P:(k + 1) * P]
                    b = wlo[:, s.mod(SPL), k * P:(k + 1) * P]
                    r = half * p.kt + k
                    pe.matmul(out, a, rhi[:, r, :], start=(r == 0), stop=False)
                    pe.matmul(out, a, rlo[:, r, :], start=False, stop=False)
                    mm = pe.matmul(out, b, rhi[:, r, :], start=False, stop=(r == q * p.kt - 1))
                mm.then_inc(blk_done, 1)

            steps(pe, lo, hi, one)

        def tile_done(eng, p, t, q=1):
            eng.wait_ge(blk_done, ((t + 1) * q + (p.own0 + SPL)).val)

        def staggered(eng, p, split, runs):
            for k in range(2):
                split(Idx(k))
            for lo, hi, evacuate in runs:
                ahead = min(hi, p.n - 2)

                def both(s):
                    split(s + 2)
                    evacuate(s)
                if ahead > lo:
                    steps(eng, lo, ahead, both)
                for k in range(max(lo, ahead), hi):
                    evacuate(Idx(k))

        def no_split(j):
            pass

        def ada_products(pe, lay):
            p = phase[f"ada{lay}"]
            if lay == 0:
                pe.wait_ge(cond_silu, 1)
            else:
                pe.wait_ge(gated, 4 * DT + 4 - 2 * DT)

            def one(j):
                b = j + p.raw0
                pe.wait_ge(raw_in[b.mod(RAW)], ((b.div(RAW) + 1) * 16).val)
                for k in range(DT):
                    mm = pe.matmul(ps[:, 5, bass.ds((j * 2).val, 2)], raw[:, b.mod(RAW), k * P:(k + 1) * P],
                                   scond[:, k, :], start=(k == 0), stop=(k == DT - 1))
                mm.then_inc(ada_used, 1)
            steps(pe, 0, p.n, one)

        def ada_params(dve, lay):
            dve.wait_ge(ada_used, 48 * (lay + 1))
            b = v("b_ada").rearrange("p (l n) -> p l n", l=2)[:, lay, :]
            dve.tensor_tensor(ada[:, lay], ps[:, 5, 0:96].rearrange("p (n c) -> p n c", c=2),
                              b.unsqueeze(2).to_broadcast([P, 48, 2]), ALU.add).then_inc(ada_ready, 1)
            dve.wait_ge(ada_ready, 3 * lay + 1)
            for part in (1, 4):
                w = ada[:, lay, part * DT:(part + 1) * DT, :]
                dve.tensor_scalar(w, w, 1.0, None, ALU.add).then_inc(ada_ready, 1)

        SEQS = ((0, P, 0), (P, TOK, 1))

        def modulate_hi(act, m):
            lay, part = m // 2, 3 * (m % 2)
            act.wait_ge(ada_ready, 3 * (lay + 1))
            for t in range(DT):
                act.wait_ge(ln_x, DT * (m - 1) + t + 1) if m else (act.wait_ge(x_in, 16) if t == 0 else None)
                for a, b, c in SEQS:
                    i = act.activation(hhi[:, t, a:b], xr[:, t, a:b], ACT.Identity,
                                       bias=ada[:, lay, part * DT + t, c:c + 1],
                                       scale=ada[:, lay, (part + 1) * DT + t, c:c + 1])
                i.then_inc(h_hi, 1)

        def modulate_lo(dve, m):
            lay, part = m // 2, 3 * (m % 2)
            dve.wait_ge(ada_ready, 3 * (lay + 1))
            for t in range(DT):
                dve.wait_ge(ln_x, DT * (m - 1) + t + 1) if m else (dve.wait_ge(x_in, 16) if t == 0 else None)
                for a, b, c in SEQS:
                    i = dve.tensor_scalar(hmod[:, t, a:b], xr[:, t, a:b], ada[:, lay, (part + 1) * DT + t, c:c + 1],
                                          ada[:, lay, part * DT + t, c:c + 1], ALU.mult, ALU.add)
                i.then_inc(h_mod, 1)
            for t in range(DT):
                dve.wait_ge(h_mod, DT * m + t + 1)
                dve.wait_ge(h_hi, DT * m + t + 1)
                dve.tensor_tensor(hlo[:, t, :], hmod[:, t, :], hhi[:, t, :].bitcast(F32), ALU.subtract).then_inc(h_lo, 1)

        def h_ready(pe, m):
            pe.wait_ge(h_hi, DT * (m + 1))
            pe.wait_ge(h_lo, DT * (m + 1))

        def norm_pe(pe, n):
            pe.wait_ge(resid, 2 + DT * (n + 1))
            for t in range(DT):
                mm = pe.matmul(ps[:, 6, 0:TOK], ones, xr[:, t, :], start=(t == 0), stop=(t == DT - 1))
            mm.then_inc(ln_mm, 1)
            for t in range(DT):
                pe.wait_ge(ln_sq, DT * n + t + 1)
                mm = pe.matmul(ps[:, 7, 0:TOK], ones, sq[:, t, :], start=(t == 0), stop=(t == DT - 1))
            mm.then_inc(ln_mm, 1)

        def norm_dve(dve, n):
            lay, j = n // 2, n % 2
            mean, std, rstd = (small[:, k * TOK:(k + 1) * TOK] for k in range(3))
            g = v("ln_g").rearrange("p (n t) -> p n t", n=4)[:, n, :]
            b = v("ln_b").rearrange("p (n t) -> p n t", n=4)[:, n, :]
            dve.wait_ge(ln_mm, 2 * n + 1)
            dve.tensor_scalar(mean, ps[:, 6, 0:TOK], 1.0 / D, None, ALU.mult).then_inc(ln_mean, 1)
            dve.wait_ge(ln_mean, n + 1)
            for t in range(DT):
                dve.tensor_tensor(xr[:, t, :], xr[:, t, :], mean, ALU.subtract).then_inc(ln_cent, 1)
            dve.wait_ge(ln_std, n + 1)
            dve.reciprocal(rstd, std).then_inc(ln_rstd, 1)
            dve.wait_ge(ln_rstd, n + 1)
            for t in range(DT):
                dve.tensor_tensor(xr[:, t, :], xr[:, t, :], rstd, ALU.mult).then_inc(ln_norm, 1)
            for t in range(DT):
                dve.wait_ge(ln_norm, DT * n + t + 1)
                dve.tensor_scalar(xr[:, t, :], xr[:, t, :], g[:, t:t + 1], b[:, t:t + 1], ALU.mult, ALU.add).then_inc(ln_x, 1)

        def norm_act(act, n):
            std = small[:, TOK:2 * TOK]
            for t in range(DT):
                act.wait_ge(ln_cent, DT * n + t + 1)
                act.activation(sq[:, t, :], xr[:, t, :], ACT.Square).then_inc(ln_sq, 1)
            act.wait_ge(ln_mm, 2 * n + 2)
            act.activation(std, ps[:, 7, 0:TOK], ACT.Sqrt, scale=1.0 / D, bias=eps[:, 0:1]).then_inc(ln_std, 1)

        def in_act(act, lay):
            p = phase[("ssd_in", "gdn_in")[lay]]
            cw = v("conv_w").rearrange("p (l t w) -> p l t w", l=2, w=3)[:, lay]
            cb = v("conv_b").rearrange("p (l t) -> p l t", l=2)[:, lay]

            def conv_centre(t):
                tile_done(act, p, t)
                act.wait_ge(conv_silu, (t + (32 * lay + 1)).val)
                act.activation(evac[:, t.mod(2), :], ps[:, t.mod(4), 0:TOK], ACT.Identity,
                               bias=cb[:, bass.ds(t.val, 1)], scale=cw[:, t.val, 1:2]).then_inc(centre, 1)

            def silu(t):
                act.wait_ge(conv_done, (t + (36 * lay + 4 + 1)).val)
                act.activation(proj[:, t.val, :], evac[:, t.mod(2), :], ACT.Silu).then_inc(conv_silu, 1)

            def conv_tile(t):
                conv_centre(t)
                silu(t + (-1))

            def gate_tile(t):
                tile_done(act, p, t)
                act.activation(proj[:, t.val, :], ps[:, t.mod(4), 0:TOK], ACT.Silu).then_inc(gate_done, 1)

            def first_gate(t):
                silu(t + (-1))
                gate_tile(t)

            staggered(act, p, lambda j: split_hi(act, p, j),
                      [(0, 1, conv_centre), (1, 32, conv_tile), (32, 33, first_gate), (33, 48, gate_tile)])

        def in_dve(dve, lay):
            cw = v("conv_w").rearrange("p (l t w) -> p l t w", l=2, w=3)[:, lay]

            def conv_taps(t):
                dve.wait_ge(centre, (t + (32 * lay + 1)).val)
                a, o = evac[:, t.mod(2), :], ps[:, t.mod(4), 0:TOK]
                for x, y in ((0, P), (P, TOK)):
                    i = dve.scalar_tensor_tensor(a[:, x + 1:y], o[:, x:y - 1], cw[:, t.val, 0:1], a[:, x + 1:y],
                                                 ALU.mult, ALU.add)
                i.then_inc(left, 1)
                dve.wait_ge(left, (t + (32 * lay + 1)).val)
                for x, y in ((0, P), (P, TOK)):
                    i = dve.scalar_tensor_tensor(a[:, x:y - 1], o[:, x + 1:y], cw[:, t.val, 2:3], a[:, x:y - 1],
                                                 ALU.mult, ALU.add)
                i.then_inc(conv_done, 1)
            steps(dve, 0, CONV_T, conv_taps)

        def in_pe(pe, lay):
            p = phase[("ssd_in", "gdn_in")[lay]]
            h_ready(pe, 2 * lay)
            multiply(pe, p, 0, 32, 1, hhi, hlo, conv_done, 36 * lay, 4)
            pe.wait_ge(conv_done, 36 * (lay + 1))
            multiply(pe, p, 32, 49, 1, hhi, hlo, gate_done, 20 * lay, 4)

        def back_pe(pe, name, n, rhi, rlo):
            p = phase[name]
            multiply(pe, p, 0, p.n, 2, rhi, rlo, gated, 10 * n, 2)

        def back_act(act, name, n):
            p, lay, part = phase[name], n // 2, 2 + 3 * (n % 2)

            def gate_out(j):
                if j.base % 2 == 0:
                    return
                t = j.div(2)
                tile_done(act, p, t, 2)
                act.wait_ge(resid, (t + (8 * n + 1)).val)
                for a, b, c in SEQS:
                    i = act.activation(evac[:, t.mod(2), a:b], ps[:, t.mod(2), a:b], ACT.Identity,
                                       scale=ada[:, lay, bass.ds((t + part * DT).val, 1), c])
                i.then_inc(gated, 1)
            staggered(act, p, lambda j: split_hi(act, p, j), [(0, p.n, gate_out)])

        def back_dve(dve, n):
            def add(t):
                dve.wait_ge(gated, (t + (10 * n + 2 + 1)).val)
                dve.scalar_tensor_tensor(xr[:, t.val, :], xr[:, t.val, :], ALPHA, evac[:, t.mod(2), :],
                                         ALU.mult, ALU.add).then_inc(resid, 1)
            steps(dve, 0, DT, add)

        def up_pe(pe, lay):
            h_ready(pe, 2 * lay + 1)
            multiply(pe, phase[f"up{lay}"], 0, 2 * FF_T, 1, hhi, hlo, up_out, 48 * lay, 4)

        def up_act(act, lay):
            p = phase[f"up{lay}"]
            fw = v("ffn_w").rearrange("p (l t w) -> p l t w", l=2, w=9)[:, lay]
            fb = v("ffn_b").rearrange("p (l t) -> p l t", l=2)[:, lay]

            def tile_centre(j):
                t = j.div(2)
                tile_done(act, p, j)
                act.wait_ge(f_silu, (t + (FF_T * lay + 1)).val)
                act.activation(evac[:, t.mod(2), :], ps[:, j.mod(4), 0:TOK], ACT.Identity,
                               bias=fb[:, bass.ds(t.val, 1)], scale=fw[:, t.val, 4:5]).then_inc(f_centre, 1)

            def hidden_hi(t):
                act.wait_ge(up_out, (t * 2 + (48 * lay + 4 + 2)).val)
                act.activation(ghi[:, t.val, :], evac[:, t.mod(2) + 4, :], ACT.Copy).then_inc(g_hi, 1)

            def silu(j):
                t = j.div(2)
                act.wait_ge(up_out, (t * 2 + (48 * lay + 4 + 1)).val)
                act.activation(evac[:, t.mod(2) + 2, :], evac[:, t.mod(2), :], ACT.Silu).then_inc(f_silu, 1)

            def evacuate(j):
                if j.base % 2:
                    silu(j)
                else:
                    tile_centre(j)
                    hidden_hi(j.div(2) + (-1))
            staggered(act, p, lambda j: split_hi(act, p, j), [(0, 1, tile_centre), (1, 2, silu), (2, p.n, evacuate)])
            hidden_hi(Idx(FF_T - 1))

        def up_dve(dve, lay):
            p = phase[f"up{lay}"]
            fw = v("ffn_w").rearrange("p (l t w) -> p l t w", l=2, w=9)[:, lay]
            taps = [(0, -1, 0), (0, -1, 1), (0, 1, 0), (0, 1, 1)] + [(r, c, 0) for r in (-1, 1) for c in (0, -1, 1)]
            behind = [None, None, 0, 1] + list(range(2, 3)) + list(range(4, 9))

            def all_taps(j):
                t = j.div(2)
                dve.wait_ge(f_centre, (t + (FF_T * lay + 1)).val)
                a, o = evac[:, t.mod(2), :], ps[:, j.mod(4), 0:TOK]
                for n, (r, c, prompt) in enumerate(taps):
                    w = fw[:, t.val, (r + 1) * 3 + c + 1:(r + 1) * 3 + c + 2]
                    c0, c1 = max(0, -c), max(0, c)
                    if prompt:
                        x, y = a[:, c0:P - c1], o[:, c0 + c:P - c1 + c]
                    else:
                        grid_a = a[:, P:TOK].rearrange("p (r c) -> p r c", c=GRID_W)
                        grid_o = o[:, P:TOK].rearrange("p (r c) -> p r c", c=GRID_W)
                        r0, r1 = max(0, -r), GRID_H - max(0, r)
                        x = grid_a[:, r0:r1, c0:GRID_W - c1]
                        y = grid_o[:, r0 + r:r1 + r, c0 + c:GRID_W - c1 + c]
                    if behind[n] is not None:
                        dve.wait_ge(f_tap, (t * 9 + (9 * FF_T * lay + behind[n] + 1)).val)
                    i = dve.scalar_tensor_tensor(x, y, w, x, ALU.mult, ALU.add)
                    i.then_inc(f_tap if n < len(taps) - 1 else up_out, 1)

            def hidden_lo(t):
                dve.wait_ge(g_hi, (t + (FF_T * lay + 2 + 1)).val)
                dve.tensor_tensor(glo[:, t.val, :], evac[:, t.mod(2) + 4, :], ghi[:, t.val, :].bitcast(F32),
                                  ALU.subtract).then_inc(g_lo, 1)

            def product(j):
                t = j.div(2)
                dve.wait_ge(f_silu, (t + (FF_T * lay + 3)).val)
                tile_done(dve, p, j)
                dve.wait_ge(g_hi, (t + (FF_T * lay + 1)).val)
                dve.tensor_tensor(evac[:, t.mod(2) + 4, :], ps[:, j.mod(4), 0:TOK], evac[:, t.mod(2) + 2, :],
                                  ALU.mult).then_inc(up_out, 1)

            def evacuate(j):
                if j.base % 2:
                    product(j)
                else:
                    all_taps(j)
                    hidden_lo(j.div(2) + (-1))
            all_taps(Idx(0))
            product(Idx(1))
            steps(dve, 2, 2 * FF_T, evacuate)
            hidden_lo(Idx(FF_T - 1))
        rows = put("rows", [P, 8, TOK], F32, at=hhi_at)
        NH = (SSD_H, GDN_H)
        NB = tuple(6 * n for n in NH)
        tok_s = small[:, 0:2 * NCH * 64].rearrange("p (k c n) -> p k c n", k=2, c=NCH)
        tok_g = small[:, 0:NCH * 64].rearrange("p (c n) -> p c n", c=NCH)
        dec_s = small[:, 384:384 + NCH * NB[0]].rearrange("p (c n) -> p c n", c=NCH)
        dec_g = small[:, 384:384 + NCH * NB[1]].rearrange("p (c n) -> p c n", c=NCH)
        wdt = small[:, 960:1152].rearrange("p (c n) -> p c n", c=NCH)
        bec = small[:, 960:960 + NCH * 32].rearrange("p (c n) -> p c n", c=NCH)
        DT_CH = 9

        def decay_act(act, lay):
            act.wait_ge(dt_abs, lay + 1)
            act.activation(rows[0:64, 2, :], rows[0:64, 1, :], ACT.Exp)
            act.activation(ea[0:64, :], v("a_log")[0:64, lay:lay + 1], ACT.Exp)
            act.activation(rows[32:64, 6, :], rows[32:64, 0, :], ACT.Exp, scale=-1.0).then_inc(dt_exp, 1)
            act.wait_ge(dt_one, lay + 1)
            act.activation(rows[0:64, 4, :], rows[0:64, 3, :], ACT.Ln).then_inc(dt_ln, 1)
            act.wait_ge(dt_cum, lay + 1)
            dec = (dec_s, dec_g)[lay]
            for c in range(NCH):
                i = act.activation(dec[:, c, :], ps[:, 6 + c // 2, (c % 2) * NB[lay]:(c % 2 + 1) * NB[lay]], ACT.Exp)
            i.then_inc(dt_dec, 1)

        def decay_dve(dve, lay):
            r = [rows[0:64, k, :] for k in range(8)]
            n = [DT_CH * lay]

            def chain(ins):
                n[0] += 1
                ins.then_inc(dt_ch, 1)
                dve.wait_ge(dt_ch, n[0])

            tile_done(dve, phase[("ssd_in", "gdn_in")[lay]], Idx(48))
            chain(dve.tensor_scalar(r[0], ps[0:64, 0, 0:TOK], v("dt_bias")[0:64, lay:lay + 1], None, ALU.add))
            dve.scalar_tensor_tensor(r[1], r[0], -1.0, r[0], ALU.mult, ALU.min).then_inc(dt_abs, 1)
            dve.wait_ge(dt_exp, lay + 1)
            dve.tensor_scalar(r[3], r[2], 1.0, None, ALU.add).then_inc(dt_one, 1)
            dve.wait_ge(dt_one, lay + 1)
            chain(dve.tensor_scalar(r[5], r[3], -1.0, None, ALU.add))
            chain(dve.tensor_scalar(r[7], r[5], 0.0, None, ALU.is_equal))
            chain(dve.tensor_tensor(r[5], r[5], r[7], ALU.add))
            chain(dve.reciprocal(r[5], r[5]))
            dve.wait_ge(dt_ln, lay + 1)
            chain(dve.tensor_tensor(r[4], r[4], r[7], ALU.add))
            chain(dve.tensor_tensor(r[4], r[4], r[2], ALU.mult))
            chain(dve.tensor_tensor(r[4], r[4], r[5], ALU.mult))
            chain(dve.scalar_tensor_tensor(r[7], r[0], 0.0, r[4], ALU.max, ALU.add))
            if lay == 0:
                dve.tensor_scalar(r[1], r[7], ea[0:64, :], -1.0, ALU.mult, ALU.mult).then_inc(dt_rows, 1)
            else:
                dve.tensor_scalar(rows[0:32, 1, :], rows[0:32, 7, :], ea[0:32, :], -1.0, ALU.mult, ALU.mult)
                dve.tensor_scalar(rows[32:64, 2, :], rows[32:64, 6, :], 1.0, None, ALU.add).then_inc(dt_one, 1)
                dve.wait_ge(dt_one, lay + 2)
                dve.reciprocal(rows[32:64, 1, :], rows[32:64, 2, :]).then_inc(dt_rows, 1)
            dve.wait_ge(dt_tr, lay + 1)
            w = (2 if lay == 0 else 1) * NCH * 64
            dve.tensor_copy(small[:, 0:w], ps[:, 1, 0:w]).then_inc(dt_tok, 1)
            dve.wait_ge(dt_dec, lay + 1)
            if lay == 0:
                dve.tensor_tensor(wdt, dec_s[:, :, 64:128], tok_s[:, 0], ALU.mult).then_inc(dt_last, 1)
            else:
                dve.tensor_tensor(bec, dec_g[:, :, 0:32], tok_g[:, :, 32:64], ALU.mult).then_inc(dt_last, 1)

        def decay_pe(pe, lay):
            pe.wait_ge(dt_rows, lay + 1)
            for k in range(2 if lay == 0 else 1):
                for c in range(NCH):
                    r = rows[0:64, (7, 1)[k] if lay == 0 else 1, c * P:(c + 1) * P]
                    mm = pe.transpose(ps[:, 1, (k * NCH + c) * 64:(k * NCH + c + 1) * 64], r, ident[0:64, 0:64])
            mm.then_inc(dt_tr, 1)
            pe.wait_ge(dt_tok, lay + 1)
            h = NH[lay]
            for c in range(NCH):
                a = tok_s[:, 1, c, :] if lay == 0 else tok_g[:, c, 0:32]
                o = ps[:, 6 + c // 2, (c % 2) * NB[lay]:(c % 2 + 1) * NB[lay]]
                for k, (m, lo, hi) in enumerate((("le", 0, h), ("ge", h, 2 * h), ("gt", 0, h), ("lt", h, 2 * h))):
                    pe.matmul(o[:, k * h:(k + 1) * h], mask(m), a[:, lo:hi], start=True, stop=True)
                mm = pe.matmul(o[:, 4 * h:6 * h], ones, a[:, 0:2 * h], start=True, stop=True)
            mm.then_inc(dt_cum, 1)

        st = [scratch0]

        def tmp(name, shape, dt=F32):
            t = put(name, shape, dt, at=st[0])
            st[0] += nbytes([P] + list(shape[1:]), dt)
            assert st[0] <= proj0, (name, st[0], proj0)
            return t

        stg = tmp("stg", [P, 2, 4, TOK])
        s0 = tmp("s0", [P, 2, 2, 256])
        xtok = tmp("xtok", [P, 2, NCH, TOK])
        seg_r = tmp("seg_r", [P, 2, 2, 512])
        e_s = tmp("e_s", [P, 2, 512])
        ge_s = tmp("ge_s", [P, 2, 2, 512])
        gm_s = tmp("gm_s", [P, NCH, 2, P])
        xw = tmp("xw", [P, 2, 4, 256])
        sdec = tmp("sdec", [P, 2, 2, 256])
        s1 = tmp("s1", [P, 2, 2, 256])
        xdt = tmp("xdt", [P, 2, 2, 256])
        inter = tmp("inter", [P, 512])
        ytok = tmp("ytok", [P, 2, 256])
        vtmp = tmp("vtmp", [P, 2, 2, P])
        st_sb = tmp("st_sb", [P, 2, 512])
        s_stg = [sem(f"s_stg{k}") for k in range(2)]
        s_out = [sem(f"s_out{k}") for k in range(2)]
        (s_a, s_xtok, s_gm, s_r, s_seg, s_exp, s_ge, s_xw, s_st, s_dec, s_new, s_stout, s_xdt, s_mm, s_yc, s_y,
         s_yt, s_vt, s_v) = (sem(x) for x in (
             "s_a", "s_xtok", "s_gm", "s_r", "s_seg", "s_exp", "s_ge", "s_xw", "s_st", "s_dec", "s_new", "s_stout",
             "s_xdt", "s_mm", "s_yc", "s_y", "s_yt", "s_vt", "s_v"))
        s_it = sem("s_it")

        def groups(eng, body):
            with eng.Fori(0, SSD_G // 2) as i:
                for b in range(2):
                    body(Idx(b, i, 2), lambda c, b=b, i=i: Idx(3 * b + c, i, 6), b)

        def tokens(c):
            return slice(c * P, (c + 1) * P)

        def heads(ap, n):
            return ap.unsqueeze(2).to_broadcast([P, 4, n])

        def h4(ap):
            return ap.rearrange("p (h n) -> p h n", h=4)

        def ssd_act(act):
            s0_in = io["s_ssd"]

            def stage(g, b):
                gg = (g if isinstance(g, int) else g.val) % SSD_G
                act.dma_start(stg[:, b, 0:2, :], proj[:, bass.ds(gg * 2, 2), :]).then_inc(s_stg[b], 16)
                act.dma_start(stg[:, b, 2, :], proj[:, gg + 16, :]).then_inc(s_stg[b], 16)
                act.dma_start(stg[:, b, 3, :], proj[:, gg + 24, :]).then_inc(s_stg[b], 16)
                act.dma_start(s0[:, b, :, :], s0_in[gg]).then_inc(s_stg[b], 16)

            act.wait_ge(conv_silu, 2 + CONV_T)
            act.wait_ge(blk_done, phase["ssd_in"].own0 + N_IN + SPL)
            act.wait_ge(dt_dec, 1)
            act.wait_ge(dt_last, 1)
            stage(0, 0)
            stage(1, 1)

            def group(g, u, b):
                act.wait_ge(s_stg[b], (g.div(2) * 64 + 64).val)
                for c in range(NCH):
                    act.wait_ge(s_a, (u(c) + 1).val)
                    act.wait_ge(s_xdt, (u(c) + 1).val)
                    act.wait_ge(s_st, (u(c) + 1).val)
                    act.activation(xtok[:, b, c, :], ps[:, c, 0:TOK], ACT.Copy).then_inc(s_xtok, 1)
                act.wait_ge(s_st, (u(0) + 7).val)
                act.wait_ge(s_out[b], (g.div(2) * 16 + 16).val)
                act.activation(st_sb[:, b, :], ps[:, 7, :], ACT.Copy).then_inc(s_stout, 1)
                for c in range(NCH):
                    act.wait_ge(s_seg, (u(c) + 3).val)
                    act.wait_ge(s_ge, (u(c) + 1).val)
                    act.activation(e_s[:, u(c).mod(2), :], ps[:, 3, :], ACT.Exp).then_inc(s_exp, 1)
                    if c == 0:
                        act.wait_ge(s_stout, (g + 1).val)
                        act.dma_start(io["o_ssd"][g.val], st_sb[:, b, :].rearrange("p (d n) -> p d n", d=2))\
                           .then_inc(s_out[b], 16)
                act.wait_ge(s_v, (u(2) + 3).val)
                stage(g + 2, b)
            groups(act, group)
            for b in range(2):
                act.wait_ge(s_stg[b], 64 * (SSD_G // 2 + 1))
                act.wait_ge(s_out[b], 16 * (SSD_G // 2 + 1))

        def ssd_pool(pool):
            pool.wait_ge(dt_last, 1)
            pool.wait_ge(blk_done, phase["ssd_in"].own0 + N_IN + SPL)

            def group(g, u, b):
                def dt_a(c, d):
                    return tok_s[:, 1, c, bass.ds((g * 4 + 32 * d).val, 4)]

                def segments(c):
                    pool.wait_ge(s_seg, (u(c) + 1).val)
                    m = ("le", "ge")
                    for d in range(2):
                        i = pool.tensor_tensor(h4(seg_r[:, u(c).mod(2), d, :]),
                                               mask(m[d]).unsqueeze(1).to_broadcast([P, 4, P]), heads(dt_a(c, d), P), ALU.mult)
                    i.then_inc(s_r, 1)

                def x_dt(c):
                    pool.wait_ge(s_xtok, (u(c) + 4).val)
                    pool.wait_ge(s_mm, (u(c) + 1).val)
                    for d in range(2):
                        i = pool.tensor_tensor(h4(xdt[:, u(c).mod(2), d, :]), h4(xtok[:, b, c, 0:256]),
                                               heads(tok_s[:, 0, c, bass.ds((g * 4 + 32 * d).val, 4)], SSD_P), ALU.mult)
                    i.then_inc(s_xdt, 1)

                def weighted(c, d, k):
                    return pool.tensor_tensor(h4(xw[:, b, k, :]), h4(xtok[:, b, c, 0:256]),
                                              heads(wdt[:, c, bass.ds((g * 4 + 32 * d).val, 4)], SSD_P), ALU.mult)

                segments(0)
                for c in range(NCH):
                    pool.wait_ge(s_xtok, (u(c) + 4).val)
                    pool.wait_ge(s_st, (u(c) + 1).val)
                    if c == CTX:
                        weighted(c, 0, 0)
                    i = weighted(c, (1, 0, 1)[c], c + 1)
                    i.then_inc(s_xw, 1)
                pool.wait_ge(s_stg[b], (g.div(2) * 64 + 64).val)
                for d in range(2):
                    pool.wait_ge(s_new, (g * 2 + (d + 1)).val)
                    pool.tensor_tensor(h4(sdec[:, b, d, :]), h4(s0[:, b, d, :]),
                                       heads(dec_s[:, 1 + d, bass.ds((g * 4 + (128 + 32 * d)).val, 4)], SSD_P),
                                       ALU.mult).then_inc(s_dec, 1)
                x_dt(0)
                segments(1)
                x_dt(1)
                segments(2)
                x_dt(2)
            groups(pool, group)

        def ssd_pe(pe):
            for s, n in ((s_seg, 2), (s_mm, 2), (s_st, 6), (s_yt, 2)):
                pe.sem_inc(s, n)

            def group(g, u, b):
                pe.wait_ge(s_stg[b], (g.div(2) * 64 + 64).val)
                for c in range(NCH):
                    pe.wait_ge(s_xtok, (u(c) + 1).val)
                    pe.wait_ge(s_gm, (u(c) + 1).val)
                    for k in range(3):
                        pe.transpose(ps[:, c, k * P:(k + 1) * P], stg[:, b, k, tokens(c)], ident)
                    pe.matmul(ps[:, c, 3 * P:4 * P], stg[:, b, 2, tokens(c)], stg[:, b, 3, tokens(c)],
                              start=True, stop=True).then_inc(s_a, 1)

                def segment(c):
                    pe.wait_ge(s_exp, (u(c) + 1).val)
                    pe.wait_ge(s_r, (u(c) + 1).val)
                    r = seg_r[:, u(c).mod(2)]
                    pe.matmul(ps[:, 3, :], mask("gt"), r[:, 0, :], start=True, stop=False)
                    pe.matmul(ps[:, 3, :], mask("lt"), r[:, 1, :], start=False, stop=True).then_inc(s_seg, 1)

                def outputs(c):
                    y = 5 + u(c).mod(2)
                    pe.wait_ge(s_v, (u(c) + 1).val)
                    pe.wait_ge(s_yc, (u(c) + 1).val)
                    pe.wait_ge(s_ge, (u(c) + 3).val)
                    pe.wait_ge(s_xdt, (u(c) + 7).val)
                    if c != CTX:
                        pe.wait_ge(s_new, (g * 2 + 6).val)
                        f, w = (s0[:, b, 0, :], s1[:, b, 1, :]) if c == LAT1 else (s1[:, b, 0, :], s0[:, b, 1, :])
                        pe.matmul(ps[:, 4, 0:256], stg[:, b, 3, tokens(c)], f, start=True, stop=True)
                        pe.matmul(ps[:, 4, 256:512], stg[:, b, 3, tokens(c)], w, start=True, stop=True)
                    for h in range(4):
                        for d in range(2):
                            mm = pe.matmul(ps[:, y, h * SSD_P:(h + 1) * SSD_P], ge_s[:, u(c).mod(2), d, h * P:(h + 1) * P],
                                           xdt[:, u(c).mod(2), d, h * SSD_P:(h + 1) * SSD_P], start=(d == 0), stop=(d == 1))
                    mm.then_inc(s_mm, 1)

                def back(c):
                    pe.wait_ge(s_y, (u(c) + 1).val)
                    for k in range(2):
                        i = pe.transpose(ps[:, 5 + u(c).mod(2), 256 + k * P:256 + (k + 1) * P],
                                         ytok[:, u(c).mod(2), k * P:(k + 1) * P], ident)
                    i.then_inc(s_yt, 1)

                segment(0)
                for c in range(NCH):
                    pe.wait_ge(s_xw, (u(c) + 1).val)
                    if c == CTX:
                        pe.wait_ge(s_new, (g * 2 + 4).val)
                    if c == LAT1:
                        pe.wait_ge(s_stout, (g + 1).val)
                    for d, k in (((0, 0), (1, 1)), ((0, 2),), ((1, 3),))[c]:
                        mm = pe.matmul(ps[:, 7, d * 256:(d + 1) * 256], xtok[:, b, c, 256:384], xw[:, b, k, :],
                                       start=True, stop=True)
                    mm.then_inc(s_st, 1)
                segment(1)
                outputs(0)
                segment(2)
                outputs(1)
                back(0)
                outputs(2)
                back(1)
                back(2)
            groups(pe, group)

        def ssd_dve(dve):
            zg, dskip = gate, v("d_skip")

            def group(g, u, b):
                for c in range(NCH):
                    dve.wait_ge(s_xtok, (u(c) + 4).val)
                    for d, m in enumerate(("le", "ge")):
                        i = dve.tensor_tensor(gm_s[:, c, d, :], ps[:, c, 3 * P:4 * P], mask(m), ALU.mult)
                    i.then_inc(s_gm, 1)

                def decayed(c):
                    dve.wait_ge(s_exp, (u(c) + 2).val)
                    dve.wait_ge(s_mm, (u(c) + 1).val)
                    dve.wait_ge(s_gm, (u(c) + 4).val)
                    for d in range(2):
                        i = dve.tensor_tensor(h4(ge_s[:, u(c).mod(2), d, :]), h4(e_s[:, u(c).mod(2), :]),
                                              gm_s[:, c, d, :].unsqueeze(1).to_broadcast([P, 4, P]), ALU.mult)
                    i.then_inc(s_ge, 1)

                def combine(c):
                    k = u(c).mod(2)
                    dve.wait_ge(s_mm, (u(c) + 3).val)
                    dve.wait_ge(s_yt, (u(c) + 1).val)
                    y = ps[:, 5 + k, 0:256]
                    if c == CTX:
                        dve.tensor_copy(ytok[:, k, :], y).then_inc(s_y, 1)
                        dve.sem_inc(s_yc, 1)
                        return
                    dve.wait_ge(s_y, u(c).val)
                    for d in range(2):
                        i = dve.tensor_tensor(h4(inter[:, d * 256:(d + 1) * 256]), h4(ps[:, 4, d * 256:(d + 1) * 256]),
                                              heads(dec_s[:, c, bass.ds((g * 4 + 32 * d).val, 4)], SSD_P), ALU.mult)
                    i.then_inc(s_yc, 1)
                    dve.wait_ge(s_yc, (u(c) + 2).val)
                    dve.tensor_tensor(inter[:, 0:256], inter[:, 0:256], inter[:, 256:512], ALU.add).then_inc(s_it, 1)
                    dve.wait_ge(s_it, (g * 2 + c).val)
                    dve.tensor_tensor(ytok[:, k, :], y, inter[:, 0:256], ALU.add).then_inc(s_y, 1)

                def gated_out(c):
                    dve.wait_ge(s_yt, (u(c) + 3).val)
                    dve.wait_ge(s_v, (u(c) + 1).val)
                    for k in range(2):
                        i = dve.scalar_tensor_tensor(vtmp[:, u(c).mod(2), k, :], stg[:, b, k, tokens(c)], dskip[:, bass.ds((g * 2 + k).val, 1)],
                                                     ps[:, 5 + u(c).mod(2), 256 + k * P:256 + (k + 1) * P], ALU.mult, ALU.add)
                    i.then_inc(s_vt, 1)
                    dve.wait_ge(s_vt, (u(c) + 1).val)
                    z = zg[:, bass.ds((g * 2).val, 2), tokens(c)]
                    dve.tensor_tensor(z, z, vtmp[:, u(c).mod(2)], ALU.mult).then_inc(s_v, 1)

                dve.wait_ge(s_st, (u(2) + 7).val)
                for d in range(2):
                    dve.wait_ge(s_dec, (g * 2 + (d + 1)).val)
                    dve.tensor_tensor(s1[:, b, d, :], sdec[:, b, d, :], ps[:, 7, d * 256:(d + 1) * 256],
                                      ALU.add).then_inc(s_new, 1)
                decayed(0)
                decayed(1)
                combine(0)
                decayed(2)
                combine(1)
                gated_out(0)
                combine(2)
                gated_out(1)
                gated_out(2)
            dve.wait_ge(gate_done, 20)
            groups(dve, group)

        def rms_act(act):
            std = small[:, 0:TOK]

            def square(t):
                act.wait_ge(rms_mm, (t + 1).val)
                act.activation(evac[:, t.mod(2) + 6, :], gate[:, t.val, :], ACT.Square).then_inc(rms_sq, 1)
            act.wait_ge(s_v, 2 + 3 * SSD_G)
            steps(act, 0, 16, square)
            act.wait_ge(rms_mm, 2 + 16)
            act.activation(std, ps[:, 7, 0:TOK], ACT.Sqrt, scale=1.0 / 2048, bias=eps[:, 1:2]).then_inc(rms_std, 1)

        def rms_pe(pe):
            pe.sem_inc(rms_mm, 2)
            for t in range(16):
                pe.wait_ge(rms_sq, t + 1)
                pe.matmul(ps[:, 7, 0:TOK], ones, evac[:, t % 2 + 6, :], start=(t == 0), stop=(t == 15)).then_inc(rms_mm, 1)

        def mixer_hi(act, lay):
            def one(t):
                if lay == 0:
                    act.wait_ge(y_scaled, (t + 1).val)
                act.activation(yhi[:, t.val, :], gate[:, t.val, :], ACT.Copy).then_inc(y_hi, 1)
            steps(act, 0, 16, one)

        def mixer_lo(dve, lay):
            rstd = small[:, TOK:2 * TOK]
            nw = v("ssd_norm")
            if lay == 0:
                dve.wait_ge(rms_std, 1)
                dve.reciprocal(rstd, small[:, 0:TOK]).then_inc(rms_rstd, 1)
                dve.wait_ge(rms_rstd, 1)

            def one(t):
                if lay == 0:
                    dve.scalar_tensor_tensor(gate[:, t.val, :], gate[:, t.val, :], nw[:, bass.ds(t.val, 1)], rstd,
                                             ALU.mult, ALU.mult).then_inc(y_scaled, 1)

            def two(t):
                dve.wait_ge(y_hi, (t + (16 * lay + 1)).val)
                dve.tensor_tensor(ylo[:, t.val, :], gate[:, t.val, :], yhi[:, t.val, :].bitcast(F32),
                                  ALU.subtract).then_inc(y_lo, 1)
            if lay == 0:
                steps(dve, 0, 16, one)
            steps(dve, 0, 16, two)

        def y_ready(pe, lay):
            pe.wait_ge(y_hi, 16 * (lay + 1))
            pe.wait_ge(y_lo, 16 * (lay + 1))
        l_sq, l_mm, l_std, l_inv, l_done = (sem(x) for x in ("l_sq", "l_mm", "l_std", "l_inv", "l_done"))

        def l2_act(act):
            def square(t):
                act.wait_ge(l_mm, (t + 1).val)
                act.activation(evac[:, t.mod(2) + 6, :], proj[:, t.val, :], ACT.Square).then_inc(l_sq, 1)

            def root(scale, bias):
                def f(t):
                    act.wait_ge(l_mm, (t + 3).val)
                    act.wait_ge(l_inv, (t + 1).val)
                    act.activation(evac[:, t.mod(2) + 4, :], ps[:, 4 + t.mod(2), 0:TOK], ACT.Sqrt, scale=scale,
                                   bias=bias).then_inc(l_std, 1)
                return f
            q_root, k_root = root(float(P), eps[:, 2:3]), root(1.0, eps[:, 1:2])
            act.wait_ge(conv_silu, 2 + 2 * CONV_T)
            square(Idx(0))
            for lo, hi, f in ((0, 8, q_root), (8, 15, k_root)):
                def both(t, f=f):
                    square(t + 1)
                    f(t)
                steps(act, lo, hi, both)
            k_root(Idx(15))

        def l2_pe(pe):
            pe.sem_inc(l_mm, 2)

            def one(t):
                pe.wait_ge(l_sq, (t + 1).val)
                pe.wait_ge(l_std, (t + 1).val)
                pe.matmul(ps[:, 4 + t.mod(2), 0:TOK], ones, evac[:, t.mod(2) + 6, :], start=True, stop=True).then_inc(l_mm, 1)
            steps(pe, 0, 16, one)

        def l2_dve(dve):
            def one(t):
                dve.wait_ge(l_std, (t + 3).val)
                dve.wait_ge(l_done, (t + 1).val)
                dve.reciprocal(evac[:, t.mod(2) + 2, :], evac[:, t.mod(2) + 4, :]).then_inc(l_inv, 1)
                dve.wait_ge(l_inv, (t + 3).val)
                dve.tensor_tensor(proj[:, t.val, :], proj[:, t.val, :], evac[:, t.mod(2) + 2, :], ALU.mult).then_inc(l_done, 1)
            steps(dve, 0, 16, one)

        st[0] = scratch0
        stq = tmp("stq", [P, 4, TOK])
        U = tmp("U", [P, NCH, 8, P])
        T_at = st[0]
        T = tmp("T", [P, NCH, 8, P])
        N_at = st[0]
        N = tmp("N", [P, NCH, 8, P])
        O_at = st[0]
        Noff = tmp("Noff", [P, NCH, 8, P])
        V_at = st[0]
        V = tmp("V", [P, NCH, 8, P])
        qk = tmp("qk", [P, NCH, 2, 512])
        vtok = tmp("vtok", [P, NCH, 512])
        vtok_at = st[0] - nbytes([P, NCH, 512], F32)
        stv = put("stv", [P, 4, TOK], F32, at=O_at)
        gr = put("gr", [P, 2, 512], F32, at=V_at)
        ge = put("ge", [P, 512], F32, at=V_at + 4096)
        gke = put("gke", [P, 512], F32, at=V_at + 6144)
        gkq = put("gkq", [P, 2, 256], F32, at=V_at + 8192)
        rhs = put("rhs", [P, 4, 512], F32, at=T_at)
        ktok = put("ktok", [P, NCH, 256], F32, at=T_at + 8192)
        bv = put("bv", [P, 6, 512], F32, at=N_at)
        vn = put("vn", [P, 6, 512], F32, at=O_at)
        S0 = put("S0", [P, 2, 512], F32, at=V_at)
        S1 = put("S1", [P, 2, 512], F32, at=V_at + 4096)
        vd = put("vd", [P, 2, 512], F32, at=V_at + 8192)
        ot = put("ot", [P, 3, 512], F32, at=vtok_at)
        (g_r, g_kkq, g_kk, g_seg, g_e, g_et, g_vt, g_vtok, g_ke, g_n, g_qk, g_off, g_w1, g_u0, g_t0, g_rst, g_v1, g_ut,
         g_u, g_t, g_bv, g_kt, g_ktok, g_tr, g_ks, g_rr, g_vn, g_vd, g_st, g_sd, g_s1, g_so, g_om, g_ss, g_rs, g_on,
         g_yt, g_v, g_c, g_sum, g_sq, g_stg, g_s0, g_sout, lev_in, lev_ready) = (sem(x) for x in (
             "g_r g_kkq g_kk g_seg g_e g_et g_vt g_vtok g_ke g_n g_qk g_off g_w1 g_u0 g_t0 g_rst g_v1 g_ut g_u g_t g_bv "
             "g_kt g_ktok g_tr g_ks g_rr g_vn g_vd g_st g_sd g_s1 g_so g_om g_ss g_rs g_on g_yt g_v g_c g_sum g_sq g_stg g_s0 "
             "g_sout lev_in lev_ready").split())
        lev32 = put("lev32", [P, 2, LEVELS, P], F32, at=top_evac)
        HG = GDN_H // 4
        TASKS = ((CTX, 0), (CTX, 1), (LAT1, 0), (LAT2, 1), (LAT2, 0), (LAT1, 1))
        SLOT = (2, 3, 0, 1, 0, 1)

        def turns(eng, body):
            with eng.Fori(0, HG) as i:
                body(i, lambda k, n: Idx(k, i, n))

        class Chain:

            def __init__(self, eng, s, i, per_turn):
                self.eng, self.s, self.i, self.per, self.n = eng, s, i, per_turn, 0

            def __call__(self, ins):
                self.n += 1
                ins.then_inc(self.s, 1)
                self.eng.wait_ge(self.s, self.i * self.per + self.n)

            def end(self):
                assert self.n == self.per, self.n

        def heads4(ap, n=P):
            return ap.unsqueeze(2).to_broadcast([P, 4, n])

        def col(t, c, first, d, i):
            return t[:, c, bass.ds(i * 4 + (first + GDN_H * d), 4)]

        def half(ap, l, odd):
            return ap.rearrange("p n (b t s) -> p n b t s", t=2, s=1 << l)[:, :, :, odd, :]

        def half1(ap, l, odd):
            return ap.rearrange("p (b t s) -> p b t s", t=2, s=1 << l)[:, :, odd, :]

        def packed(ap, l):
            return ap.rearrange("p (n b s) -> p n b s", n=4, s=1 << l)

        def gdn_act(act):
            act.wait_ge(dt_last, 2)
            act.wait_ge(l_done, 2 + 16)
            act.wait_ge(gate_done, 40)

            def turn(i, at):
                act.wait_ge(g_v, at(1, 3).val)
                act.wait_ge(g_sout, at(16, 32).val)
                act.dma_start(stq[:, 0:2, :], proj[:, bass.ds(i * 2 + 8, 2), :]).then_inc(g_stg, 16)
                act.dma_start(stq[:, 2:4, :], proj[:, bass.ds(i * 2, 2), :]).then_inc(g_stg, 16)
                act.dma_start(stv[:, :, :], proj[:, bass.ds(i * 4 + 16, 4), :]).then_inc(g_stg, 16)
                for c in range(NCH):
                    u = at(c, 3)
                    act.wait_ge(g_seg, (u + 2).val)
                    act.wait_ge(g_n, (u + 1).val)
                    act.wait_ge(g_et, (u + 1).val)
                    act.activation(ge[:, :], ps[:, 7, :], ACT.Exp).then_inc(g_e, 1)
                    act.wait_ge(g_vt, (u + 1).val)
                    act.activation(vtok[:, c, :], ps[:, 2 * c + 1, :], ACT.Copy).then_inc(g_vtok, 1)
                for l in range(1, LEVELS):
                    for c in range(NCH):
                        act.wait_ge(g_ut, at(3 * (l - 1) + c + 1, 18).val)
                        for d in range(2):
                            a = act.activation(half(U[:, c, 4 * d:4 * d + 4, :], l, 1 - d),
                                               packed(ps[:, 2 * c + 1, 256 * d:256 * d + 256], l), ACT.Copy)
                        a.then_inc(g_u, 1)
                        if l < LEVELS - 1:
                            for d in range(2):
                                a = act.activation(half(T[:, c, 4 * d:4 * d + 4, :], l, d),
                                                   packed(ps[:, 2 * c, 256 * d:256 * d + 256], l), ACT.Copy)
                            a.then_inc(g_t, 1)
                act.dma_start(S0[:, :, :], io["s_gdn"][i]).then_inc(g_s0, 16)
                act.wait_ge(g_kt, at(1, 2).val)
                act.activation(ktok[:, 0:2, :], ps[:, 6, :].rearrange("p (c n) -> p c n", c=2), ACT.Copy)
                act.wait_ge(g_kt, at(2, 2).val)
                act.activation(ktok[:, 2, :], ps[:, 7, 0:256], ACT.Copy).then_inc(g_ktok, 1)

                def solved(q):
                    act.wait_ge(g_tr, at(q + 1, 6).val)
                    act.activation(vn[:, q, :], ps[:, (0, 1, 4, 5, 4, 5)[q], :], ACT.Copy).then_inc(g_vn, 1)

                def state_out(q):
                    act.wait_ge(g_st, at(q + 1, 4).val)
                    act.activation(rhs[:, SLOT[q], :], ps[:, 6 + q, :], ACT.Copy).then_inc(g_so, 1)
                for q in range(4):
                    solved(q)
                for q in range(2):
                    state_out(q)
                for q in range(2):
                    act.wait_ge(g_so, at(q + 1, 2).val)
                    act.dma_start(io["o_gdn"][i][:, q, :], rhs[:, SLOT[q], :]).then_inc(g_sout, 16)
                solved(4)
                solved(5)
            turns(act, turn)
            act.wait_ge(g_v, 1 + 3 * HG)
            act.wait_ge(g_sout, 16 + 32 * HG)

        def gdn_pool(pool):
            pool.wait_ge(lev_ready, 1)

            def turn(i, at):
                pool.wait_ge(g_stg, at(48, 48).val)
                pool.wait_ge(g_vn, at(1, 6).val)
                for c in range(NCH):
                    pool.wait_ge(g_seg, at(c + 1, 3).val)
                    for d, m in enumerate(("gt", "lt")):
                        a = pool.tensor_tensor(h4(gr[:, d, :]), mask(m).unsqueeze(1).to_broadcast([P, 4, P]),
                                               heads4(col(tok_g, c, 0, d, i)), ALU.mult)
                    a.then_inc(g_r, 1)

                def off(l, c):
                    for d in range(2):
                        a = pool.tensor_tensor(Noff[:, c, 4 * d:4 * d + 4, :], N[:, c, 4 * d:4 * d + 4, :],
                                               level[:, d, l, :].unsqueeze(1).to_broadcast([P, 4, P]), ALU.mult)
                    a.then_inc(g_off, 1)
                for c in range(NCH):
                    pool.wait_ge(g_vt, at(3, 3).val)
                    pool.wait_ge(g_n, at(c + 2, 3).val)
                    off(0, c)
                for c in range(NCH):
                    pool.wait_ge(g_off, at(c + 1, 21).val)
                    for d in range(2):
                        a = pool.tensor_tensor(T[:, c, 4 * d:4 * d + 4, :], Noff[:, c, 4 * d:4 * d + 4, :],
                                               ident.unsqueeze(1).to_broadcast([P, 4, P]), ALU.add)
                    a.then_inc(g_t0, 1)
                for l in range(1, LEVELS):
                    for c in range(NCH):
                        pool.wait_ge(g_w1, at(3 * (l - 1) + c + 1, 21).val)
                        if l == 1:
                            pool.wait_ge(g_t0, at(c + 1, 3).val)
                        off(l, c)
                pool.wait_ge(g_off, at(21, 21).val)
                for q, (c, d) in enumerate(TASKS):
                    pool.wait_ge(g_vtok, at(c + 1, 3).val)
                    pool.tensor_tensor(h4(bv[:, q, :]), h4(vtok[:, c, :]), heads4(col(tok_g, c, 32, d, i)),
                                       ALU.mult).then_inc(g_bv, 1)
                pool.wait_ge(g_s0, at(16, 16).val)
                for d in range(2):
                    pool.tensor_tensor(h4(S1[:, d, :]), h4(S0[:, d, :]), heads4(col(dec_g, 1 + d, 64, d, i)),
                                       ALU.mult).then_inc(g_sd, 1)
                for c in range(NCH):
                    pool.wait_ge(g_ss, at(c + 1, 3).val)
                    pool.tensor_tensor(ss[:, c, 2, :], ss[:, c, 1, :], eps[:, 3:4].to_broadcast([P, 4]), ALU.pow).then_inc(g_rs, 1)
            turns(pool, turn)

        def gdn_pe(pe):
            for s, n in ((g_seg, 1), (g_et, 1)):
                pe.sem_inc(s, n)

            def turn(i, at):
                pe.wait_ge(g_stg, at(48, 48).val)
                pe.wait_ge(g_v, at(1, 3).val)
                for c in range(NCH):
                    tk = tokens(c)
                    pe.wait_ge(g_kk, at(c + 1, 3).val)
                    for k in range(2):
                        mm = pe.matmul(ps[:, 6, k * 256:(k + 1) * 256].rearrange("p (t n) -> p t n", t=2),
                                       stq[:, k, tk], stq[:, k:k + 3:2, tk], start=True, stop=True)
                    mm.then_inc(g_kkq, 1)
                    pe.wait_ge(g_e, at(c + 1, 3).val)
                    pe.wait_ge(g_r, at(c + 1, 3).val)
                    pe.matmul(ps[:, 7, :], mask("le"), gr[:, 0, :], start=True, stop=False)
                    pe.matmul(ps[:, 7, :], mask("ge"), gr[:, 1, :], start=False, stop=True).then_inc(g_seg, 1)
                    for h in range(4):
                        mm = pe.transpose(ps[:, 2 * c + 1, h * P:(h + 1) * P], stv[:, h, tk], ident)
                    mm.then_inc(g_vt, 1)
                    pe.wait_ge(g_e, at(c + 2, 3).val)
                    for h in range(4):
                        mm = pe.transpose(ps[:, 2 * c, h * P:(h + 1) * P], ge[:, h * P:(h + 1) * P], ident)
                    mm.then_inc(g_et, 1)
                for c in range(NCH):
                    pe.wait_ge(g_off, at(c + 1, 21).val)
                    pe.wait_ge(g_qk, at(c + 1, 3).val)
                    pe.wait_ge(g_vtok, at(c + 1, 3).val)
                    for n in range(8):
                        mm = pe.transpose(ps[:, 2 * c + n // 4, (n % 4) * P:(n % 4 + 1) * P], Noff[:, c, n, :], ident)
                    mm.then_inc(g_w1, 1)
                for l in range(1, LEVELS):
                    for c in range(NCH):
                        pe.wait_ge(g_off, at(3 * l + c + 1, 21).val)
                        if l == 1:
                            pe.wait_ge(g_u0, at(c + 1, 3).val)
                        else:
                            pe.wait_ge(g_u, at(3 * (l - 2) + c + 1, 18).val)
                            pe.wait_ge(g_t, at(3 * (l - 2) + c + 1, 15).val)
                        for n in range(8):
                            d = n // 4
                            mm = pe.matmul(ps[:, 2 * c, n * 64:(n + 1) * 64], Noff[:, c, n, :], half1(U[:, c, n, :], l, 1 - d),
                                           start=True, stop=True)
                        mm.then_inc(g_w1, 1)
                    for c in range(NCH):
                        pe.wait_ge(g_v1, at(3 * (l - 1) + c + 1, 18).val)
                        if l == 1:
                            pe.wait_ge(g_t0, at(c + 1, 3).val)
                        for n in range(8):
                            d = n // 4
                            mm = pe.matmul(ps[:, 2 * c + 1, n * 64:(n + 1) * 64], T[:, c, n, :], half1(V[:, c, n, :], l, 1 - d),
                                           start=True, stop=True)
                        if l < LEVELS - 1:
                            for n in range(8):
                                d = n // 4
                                mm = pe.matmul(ps[:, 2 * c, n * 64:(n + 1) * 64], V[:, c, n, :], half1(T[:, c, n, :], l, d),
                                               start=True, stop=True)
                        mm.then_inc(g_ut, 1)
                for c in range(NCH):
                    for k in range(2):
                        mm = pe.transpose(ps[:, 6 + c // 2, (c % 2) * 256 + k * P:(c % 2) * 256 + (k + 1) * P],
                                          stq[:, k, tokens(c)], ident)
                    if c:
                        mm.then_inc(g_kt, 1)

                def solve(q, r):
                    c, d = TASKS[q]
                    for h in range(4):
                        mm = pe.matmul(ps[:, (0, 1, 4, 5, 4, 5)[q], h * P:(h + 1) * P], U[:, c, 4 * d + h, :],
                                       r[:, h * P:(h + 1) * P], start=True, stop=True)
                    mm.then_inc(g_tr, 1)

                def state_read(q, s):
                    c, d = TASKS[q]
                    for k in range(2):
                        mm = pe.matmul(ps[:, 2 + d, k * 256:(k + 1) * 256], stq[:, k, tokens(c)], s[:, k * 256:(k + 1) * 256],
                                       start=True, stop=True)
                    mm.then_inc(g_ks, 1)

                def state_add(q):
                    c, d = TASKS[q]
                    pe.wait_ge(g_vd, at(q + 1, 4).val)
                    for k in range(2):
                        mm = pe.matmul(ps[:, 6 + d, k * 256:(k + 1) * 256], ktok[:, c, k * P:(k + 1) * P],
                                       vd[:, q % 2, k * 256:(k + 1) * 256], start=True, stop=True)
                    mm.then_inc(g_st, 1)

                def outputs(c):
                    b = (0, 1, 4)[c]
                    if c != CTX:
                        pe.wait_ge(g_s1, at(2, 2).val)
                        f, w = (S0[:, 0], S1[:, 1]) if c == LAT1 else (S1[:, 0], S0[:, 1])
                        for k in range(2):
                            for bank, s in ((b + 1, f), (b + 2, w)):
                                pe.matmul(ps[:, bank, k * 256:(k + 1) * 256], stq[:, 2 + k, tokens(c)],
                                          s[:, k * 256:(k + 1) * 256], start=True, stop=True)
                    for h in range(4):
                        for d in range(2):
                            q = TASKS.index((c, d))
                            mm = pe.matmul(ps[:, b, h * P:(h + 1) * P], qk[:, c, d, h * P:(h + 1) * P],
                                           vn[:, q, h * P:(h + 1) * P], start=(d == 0), stop=(d == 1))
                    mm.then_inc(g_om, 1)

                def back(c):
                    pe.wait_ge(g_on, at(c + 1, 3).val)
                    pe.wait_ge(g_v, at(c + 1, 3).val)
                    for h in range(4):
                        mm = pe.transpose(ps[:, 7, h * P:(h + 1) * P], ot[:, 2, h * P:(h + 1) * P], ident)
                    mm.then_inc(g_yt, 1)

                pe.wait_ge(g_u, at(18, 18).val)
                for q in range(2):
                    pe.wait_ge(g_bv, at(q + 1, 6).val)
                    solve(q, bv[:, q])
                pe.wait_ge(g_s0, at(16, 16).val)
                for q in (2, 3):
                    state_read(q, S0[:, TASKS[q][1]])
                for q in (2, 3):
                    pe.wait_ge(g_rr, at(q - 1, 4).val)
                    solve(q, rhs[:, SLOT[q]])
                pe.wait_ge(g_ktok, at(1, 1).val)
                state_add(0)
                state_add(1)
                for q in (2, 3):
                    pe.wait_ge(g_so, at(q - 1, 2).val)
                    state_add(q)
                outputs(CTX)
                for q in (4, 5):
                    pe.wait_ge(g_s1, at(TASKS[q][1] + 1, 2).val)
                    state_read(q, S1[:, TASKS[q][1]])
                for q in (4, 5):
                    pe.wait_ge(g_rr, at(q - 1, 4).val)
                    pe.wait_ge(g_vn, at(q, 6).val)
                    solve(q, rhs[:, SLOT[q]])
                back(CTX)
                pe.wait_ge(g_vn, at(7, 6).val)
                outputs(LAT1)
                outputs(LAT2)
                back(LAT1)
                back(LAT2)
            turns(pe, turn)

        def gdn_dve(dve):
            nw = v("gdn_norm")

            def turn(i, at):
                chain = Chain(dve, g_c, i, 11)

                def kpair(t):
                    return ps[:, 6, :].rearrange("p (k t n) -> p k t n", k=2, t=2)[:, :, t, :]

                for c in range(NCH):
                    u = at(c, 3)
                    dve.wait_ge(g_kkq, (u + 1).val)
                    dve.wait_ge(g_e, (u + 2).val)
                    dve.wait_ge(g_n, (u + 1).val)
                    dve.tensor_tensor(gke[:, :].rearrange("p (k r n) -> p k r n", k=2, r=2),
                                      kpair(0).unsqueeze(2).to_broadcast([P, 2, 2, P]),
                                      ge[:, :].rearrange("p (k r n) -> p k r n", k=2, r=2), ALU.mult).then_inc(g_ke, 1)
                    dve.wait_ge(g_qk, at(c, 3).val) if c else None
                    for d, m in enumerate(("le", "ge")):
                        a = dve.tensor_tensor(gkq[:, d, :].rearrange("p (k n) -> p k n", k=2), kpair(1),
                                              mask(m).unsqueeze(1).to_broadcast([P, 2, P]), ALU.mult)
                    a.then_inc(g_kk, 1)
                    dve.wait_ge(g_ke, (u + 1).val)
                    for d in range(2):
                        a = dve.scalar_tensor_tensor(N[:, c, 4 * d:4 * d + 4, :], h4(gke[:, :]), -1.0,
                                                     heads4(col(tok_g, c, 32, d, i)), ALU.mult, ALU.mult)
                    a.then_inc(g_n, 1)
                    dve.wait_ge(g_et, (u + 2).val)
                    dve.wait_ge(g_kk, (u + 2).val)
                    for d in range(2):
                        a = dve.tensor_tensor(qk[:, c, d, :].rearrange("p (k r n) -> p k r n", k=2, r=2),
                                              ps[:, 2 * c, :].rearrange("p (k r n) -> p k r n", k=2, r=2),
                                              gkq[:, d, :].rearrange("p (k n) -> p k n", k=2).unsqueeze(2)
                                              .to_broadcast([P, 2, 2, P]), ALU.mult)
                    a.then_inc(g_qk, 1)
                for c in range(NCH):
                    dve.wait_ge(g_w1, at(c + 1, 21).val)
                    for d in range(2):
                        a = dve.tensor_tensor(U[:, c, 4 * d:4 * d + 4, :], h4(ps[:, 2 * c + d, :]),
                                              ident.unsqueeze(1).to_broadcast([P, 4, P]), ALU.add)
                    a.then_inc(g_u0, 1)
                for l in range(1, LEVELS):
                    for c in range(NCH):
                        if l == 1:
                            dve.wait_ge(g_n, at(4, 3).val)
                            dve.wait_ge(g_qk, at(3, 3).val)
                        else:
                            dve.wait_ge(g_ut, at(3 * (l - 2) + c + 1, 18).val)
                        for d in range(2):
                            a = dve.tensor_copy(half(V[:, c, 4 * d:4 * d + 4, :], l, d),
                                                half1(ident, l, d).unsqueeze(1).to_broadcast([P, 4, 64 >> l, 1 << l]))
                        a.then_inc(g_rst, 1)
                        dve.wait_ge(g_w1, at(3 * l + c + 1, 21).val)
                        for d in range(2):
                            a = dve.tensor_tensor(half(V[:, c, 4 * d:4 * d + 4, :], l, 1 - d),
                                                  packed(ps[:, 2 * c, 256 * d:256 * d + 256], l),
                                                  half1(ident, l, 1 - d).unsqueeze(1).to_broadcast([P, 4, 64 >> l, 1 << l]),
                                                  ALU.add)
                        a.then_inc(g_v1, 1)

                def right_side(q):
                    c, d = TASKS[q]
                    dve.wait_ge(g_ks, at(q - 1, 4).val)
                    dve.wait_ge(g_bv, at(q + 1, 6).val)
                    r = rhs[:, SLOT[q], :]
                    if q >= 4:
                        dve.wait_ge(g_tr, at(q - 1, 6).val)
                    chain(dve.tensor_tensor(h4(r), h4(ps[:, 2 + d, :]), heads4(col(bec, c, 0, d, i)), ALU.mult))
                    dve.tensor_tensor(r, bv[:, q, :], r, ALU.subtract).then_inc(g_rr, 1)

                def decayed(q):
                    c, d = TASKS[q]
                    dve.wait_ge(g_vn, at(q + 2, 6).val)
                    if q >= 2:
                        dve.wait_ge(g_st, at(q - 1, 4).val)
                    dve.tensor_tensor(h4(vd[:, q % 2, :]), h4(vn[:, q, :]), heads4(col(dec_g, c, 32, d, i)),
                                      ALU.mult).then_inc(g_vd, 1)

                def total(c):
                    b = (0, 1, 4)[c]
                    o, t = ot[:, 0, :], ot[:, 1, :]
                    dve.wait_ge(g_om, at(c + 1, 3).val)
                    if c == CTX:
                        dve.wait_ge(g_bv, at(6, 6).val)
                        chain(dve.tensor_copy(o, ps[:, b, :]))
                    else:
                        dve.wait_ge(g_on, at(c, 3).val)
                        dve.tensor_tensor(h4(o), h4(ps[:, b + 1, :]), heads4(col(dec_g, c, 0, 0, i)), ALU.mult)
                        chain(dve.tensor_tensor(h4(t), h4(ps[:, b + 2, :]), heads4(col(dec_g, c, 0, 1, i)), ALU.mult))
                        chain(dve.tensor_tensor(o, o, t, ALU.add))
                        chain(dve.tensor_tensor(o, o, ps[:, b, :], ALU.add))
                    dve.tensor_tensor(t, o, o, ALU.mult).then_inc(g_sq, 1)
                    dve.wait_ge(g_sq, at(c + 1, 3).val)
                    dve.tensor_reduce(ss[:, c, 0, :], h4(t), AX_X, ALU.add).then_inc(g_sum, 1)
                    dve.wait_ge(g_sum, at(c + 1, 3).val)
                    dve.tensor_scalar(ss[:, c, 1, :], ss[:, c, 0, :], 1.0 / P, RMS_EPS, ALU.mult, ALU.add).then_inc(g_ss, 1)

                def normed(c):
                    dve.wait_ge(g_rs, at(c + 1, 3).val)
                    if c:
                        dve.wait_ge(g_yt, at(c, 3).val)
                    dve.tensor_tensor(h4(ot[:, 2, :]), h4(ot[:, 0, :]), heads4(ss[:, c, 2, :]), ALU.mult).then_inc(g_on, 1)

                def gated_out(c):
                    dve.wait_ge(g_yt, at(c + 1, 3).val)
                    z = gate[:, bass.ds(i * 4, 4), tokens(c)]
                    dve.scalar_tensor_tensor(z, h4(ps[:, 7, :]), nw[:, 0:1], z, ALU.mult, ALU.mult).then_inc(g_v, 1)

                right_side(2)
                right_side(3)
                for q in range(4):
                    decayed(q)
                for d in range(2):
                    dve.wait_ge(g_st, at(3 + d, 4).val)
                    dve.wait_ge(g_sd, at(d + 1, 2).val)
                    dve.tensor_tensor(S1[:, d, :], S1[:, d, :], ps[:, 6 + d, :], ALU.add).then_inc(g_s1, 1)
                total(CTX)
                right_side(4)
                right_side(5)
                normed(CTX)
                gated_out(CTX)
                total(LAT1)
                normed(LAT1)
                total(LAT2)
                gated_out(LAT1)
                normed(LAT2)
                gated_out(LAT2)
                chain.end()
            turns(dve, turn)
        block = ctx.enter_context(nc.Block())

        @block.sync
        def _(sp):
            sp.dma_start(vec[:], io["vec"]).then_inc(consts_in, 16)
            sp.dma_start(masks[:], io["masks"]).then_inc(consts_in, 16)
            sp.dma_start(lev32[:], io["level"]).then_inc(lev_in, 16)
            sp.dma_start(xr[:], io["x"]).then_inc(x_in, 16)
            for p in order:
                load_weights(sp, p)
            sp.wait_ge(ln_x, 2 * DEPTH * DT)
            sp.dma_start(io["y"], xr[:]).then_inc(out_done, 16)
            sp.wait_ge(out_done, 16)
            for b in range(2):
                sp.wait_ge(s_out[b], 16 * (SSD_G // 2 + 1))

        @block.gpsimd
        def _(pool):
            for lay in range(DEPTH):
                split_lo(pool, phase[("ssd_in", "gdn_in")[lay]])
                (ssd_pool, gdn_pool)[lay](pool)
                for name in (("ssd_out", "gdn_out")[lay], f"up{lay}", f"down{lay}"):
                    split_lo(pool, phase[name])

        @block.scalar
        def _(act):
            act.sem_inc(g_hi, 2)
            for s, n in ((s_xtok, 3), (s_exp, 1), (conv_silu, 2), (f_silu, 2), (l_std, 2), (g_e, 1), (g_vn, 1),
                         (g_sout, 16)):
                act.sem_inc(s, n)
            act.wait_ge(consts_in, 32)
            act.wait_ge(lev_in, 16)
            act.activation(level[:], lev32[:], ACT.Copy).then_inc(lev_ready, 1)
            act.activation(scond[:], cond, ACT.Silu).then_inc(cond_silu, 1)
            for lay in range(DEPTH):
                modulate_hi(act, 2 * lay)
                in_act(act, lay)
                decay_act(act, lay)
                if lay == 0:
                    ssd_act(act)
                    rms_act(act)
                else:
                    l2_act(act)
                    gdn_act(act)
                mixer_hi(act, lay)
                back_act(act, ("ssd_out", "gdn_out")[lay], 2 * lay)
                norm_act(act, 2 * lay)
                modulate_hi(act, 2 * lay + 1)
                up_act(act, lay)
                back_act(act, f"down{lay}", 2 * lay + 1)
                norm_act(act, 2 * lay + 1)

        @block.tensor
        def _(pe):
            pe.sem_inc(blk_done, SPL)
            pe.wait_ge(consts_in, 32)
            for lay in range(DEPTH):
                ada_products(pe, lay)
                in_pe(pe, lay)
                decay_pe(pe, lay)
                if lay == 0:
                    ssd_pe(pe)
                    rms_pe(pe)
                else:
                    l2_pe(pe)
                    gdn_pe(pe)
                y_ready(pe, lay)
                back_pe(pe, ("ssd_out", "gdn_out")[lay], 2 * lay, yhi, ylo)
                norm_pe(pe, 2 * lay)
                up_pe(pe, lay)
                pe.wait_ge(g_hi, 2 + FF_T * (lay + 1))
                pe.wait_ge(g_lo, FF_T * (lay + 1))
                back_pe(pe, f"down{lay}", 2 * lay + 1, ghi, glo)
                norm_pe(pe, 2 * lay + 1)

        @block.vector
        def _(dve):
            for s, n in ((resid, 2), (s_gm, 3), (s_ge, 2), (s_xdt, 6), (s_new, 4), (s_yc, 1), (s_v, 2),
                         (s_out[0], 16), (s_out[1], 16),
                         (l_inv, 2), (l_done, 2), (g_kk, 1), (g_n, 1), (g_v, 1)):
                dve.sem_inc(s, n)
            dve.wait_ge(consts_in, 32)
            for lay in range(DEPTH):
                ada_params(dve, lay)
                modulate_lo(dve, 2 * lay)
                in_dve(dve, lay)
                decay_dve(dve, lay)
                if lay == 0:
                    ssd_dve(dve)
                else:
                    l2_dve(dve)
                    gdn_dve(dve)
                mixer_lo(dve, lay)
                back_dve(dve, 2 * lay)
                norm_dve(dve, 2 * lay)
                modulate_lo(dve, 2 * lay + 1)
                up_dve(dve, lay)
                back_dve(dve, 2 * lay + 1)
                norm_dve(dve, 2 * lay + 1)


def layouts(q):
    import numpy as np
    f = {k: np.asarray(a) for k, a in q.items()}

    def cols(a):
        a = a.reshape(a.shape[:-1] + (-1, P))
        return np.moveaxis(a, -1, 0)

    def blocks(w, kt, q):
        w = np.pad(w, ((0, 0), (0, -w.shape[1] % P)))
        m = w.shape[1] // P
        w = w.reshape(q, kt, P, m, P)
        return np.ascontiguousarray(w.transpose(3, 0, 2, 1, 4)).reshape(m * q, P, kt * P)

    vec = np.zeros((P, NVEC), np.float32)

    def fill(name, a):
        lo, hi = VEC[name]
        a = a.reshape(a.shape[0], -1)
        vec[:a.shape[0], lo:hi] = a
    fill("b_ada", cols(f["b_ada"]))
    fill("ln_g", cols(f["ln_g"]))
    fill("ln_b", cols(f["ln_b"]))
    cw = np.stack([f["ssd_conv_w"][0], f["gdn_conv_w"][0]])
    fill("conv_w", cols(cw).transpose(0, 1, 3, 2))
    cb = np.zeros((2, CONV_T * P), np.float32)
    cb[0] = f["ssd_conv_b"][0]
    fill("conv_b", cols(cb))
    for name, s, g in (("dt_bias", "ssd_dt_bias", "gdn_dt_bias"), ("a_log", "ssd_a_log", "gdn_a_log")):
        a = np.zeros((P, 2), np.float32)
        a[:64, 0] = f[s].reshape(-1)
        a[:32, 1] = f[g].reshape(-1)
        fill(name, a)
    fill("d_skip", cols(np.repeat(f["ssd_d"][0], SSD_P)))
    fill("ssd_norm", cols(f["ssd_norm_w"][0]))
    fill("gdn_norm", f["gdn_norm_w"][0].reshape(P, 1))
    fill("ffn_w", cols(f["ffn_conv_w"]).transpose(0, 1, 4, 2, 3))
    fill("ffn_b", cols(f["ffn_conv_b"]))
    fill("cond", cols(np.stack([f["c_ctx"], f["c"][0]])).transpose(0, 2, 1))
    vec[:, VEC["eps"][0]:VEC["eps"][1]] = np.array([LN_EPS, RMS_EPS, P * RMS_EPS, -0.5], np.float32)

    p, n = np.arange(P)[:, None], np.arange(P)[None, :]
    masks = np.stack([p == n, p <= n, p >= n, p > n, p < n, p >= 0 * n], 1).astype(np.float32)
    lev = np.zeros((P, 2, LEVELS, P), np.float32)
    for l in range(LEVELS):
        s = 1 << l
        pair, odd = (p >> (l + 1)) == (n >> (l + 1)), ((p // s) % 2 == 1) & ((n // s) % 2 == 0)
        lev[:, 0, l] = pair & odd
        lev[:, 1, l] = (pair & odd).T
    x = np.concatenate([f["x_prompt"][0], f["x_sample"][0]], 0)

    sin, gin = f["ssd_w_in"][0], f["gdn_w_in"][0]
    sin = np.concatenate([sin[:, 2048:6144], sin[:, :2048], sin[:, 6144:]], 1)
    up = []
    for w in f["ffn_w_up"]:
        a = blocks(w, KT_IN, 1)
        up.append(np.stack([a[:FF_T], a[FF_T:]], 1).reshape(2 * FF_T, P, KT_IN * P))
    s_ssd = np.stack([f["state_ssd_fwd"][0, 0], f["state_ssd_bwd"][0, 0]])
    s_ssd = s_ssd.reshape(2, SSD_G, 256, P).transpose(1, 3, 0, 2)
    s_gdn = np.stack([f["state_gdn_fwd"][0, 0], f["state_gdn_bwd"][0, 0]])
    s_gdn = s_gdn.reshape(2, 4, 4, P, P).transpose(1, 3, 0, 2, 4)
    out = {
        "vec": vec, "masks": masks, "level": lev, "x": cols(x).transpose(0, 2, 1),
        "s_ssd": s_ssd, "s_gdn": s_gdn.reshape(4, P, 2, 512),
        "w_ada0": blocks(f["w_ada"][0], KT_IN, 1), "w_ada1": blocks(f["w_ada"][1], KT_IN, 1),
        "w_in0": blocks(sin, KT_IN, 1), "w_in1": blocks(gin, KT_IN, 1),
        "w_out0": blocks(f["ssd_w_out"][0], KT_IN, 2), "w_out1": blocks(f["gdn_w_out"][0], KT_IN, 2),
        "w_up0": up[0], "w_up1": up[1],
        "w_down0": blocks(f["ffn_w_down"][0], KT_DOWN, 2), "w_down1": blocks(f["ffn_w_down"][1], KT_DOWN, 2),
    }
    return {k: np.ascontiguousarray(a) for k, a in out.items()}


def kernel(**inputs):
    import numpy as np
    import concourse.bacc as bacc
    from concourse.bass_utils import run_bass_kernel_spmd as run

    nc = bacc.Bacc("TRN2", target_bir_lowering=False, num_devices=1)
    arrays, dram = {}, {}
    for name, a in layouts(inputs).items():
        arrays[name + "_in"] = a
        dram[name] = nc.dram_tensor(name + "_in", a.shape, F32, kind="ExternalInput").ap()
    for k in ("w_ada", "w_in", "w_out", "w_up", "w_down"):
        dram[k] = [dram.pop(k + "0"), dram.pop(k + "1")]
    for name, shape in (("y", (P, DT, TOK)), ("o_ssd", (SSD_G, P, 2, 256)), ("o_gdn", (4, P, 2, 512))):
        dram[name] = nc.dram_tensor(name + "_out", shape, F32, kind="ExternalOutput").ap()
    trunk(nc, dram)
    r = run(nc, [arrays], core_ids=[0]).results[0]
    y = r["y_out"].transpose(2, 1, 0).reshape(TOK, D)
    s = r["o_ssd_out"].transpose(2, 0, 3, 1).reshape(2, 1, 1, SSD_H, SSD_P, P)
    g = r["o_gdn_out"].reshape(4, P, 2, 4, P).transpose(2, 0, 3, 1, 4).reshape(2, 1, 1, GDN_H, P, P)
    got = (y[None, :P], y[None, P:], s[0], s[1], g[0], g[1])
    return tuple(np.ascontiguousarray(a) for a in got)
```

```python
from contextlib import ExitStack

import concourse.bass as bass
from concourse import mybir

F32 = mybir.dt.float32
F32R = mybir.dt.float32r
BF16 = mybir.dt.bfloat16
ALU = mybir.AluOpType
ACT = mybir.ActivationFunctionType
AX_X = mybir.AxisListType.X

P = 128
DEPTH = 2
D = 1024
DT = D // P
TOK = 384
NCH = TOK // P
CTX, LAT1, LAT2 = range(NCH)
GRID_W = 64
GRID_H = 256 // GRID_W
N_IN = 49
CONV_T = 32
GATE_T = 16
N_OUT = 2 * DT
FF = 2816
FF_T = FF // P
N_DOWN = 2 * DT
KT_IN = DT
KT_DOWN = FF_T // 2
ADA_T = 6 * DT
ALPHA = 4.0 ** 0.25
LN_EPS = 1e-5
RMS_EPS = 1e-6
SSD_H, SSD_P, SSD_G = 32, 64, 8
GDN_H, GDN_KH = 16, 8
LEVELS = 7
RAW = 4
ADA_1 = 2 * DT
SPL = 2

VEC = {}
_at = 0
for _name, _n in (("b_ada", 2 * 48), ("ln_g", 2 * 2 * DT), ("ln_b", 2 * 2 * DT), ("conv_w", 2 * CONV_T * 3),
                  ("conv_b", 2 * CONV_T), ("dt_bias", 2), ("a_log", 2), ("d_skip", 16), ("ssd_norm", 16),
                  ("gdn_norm", 1), ("ffn_w", 2 * FF_T * 9), ("ffn_b", 2 * FF_T), ("cond", DT * 2), ("eps", 4)):
    VEC[_name] = (_at, _at + _n)
    _at += _n
NVEC = _at
MASKS = ("ident", "le", "ge", "gt", "lt", "ones")


class Idx:

    def __init__(self, base, i=None, step=0):
        self.base, self.i, self.step = base, i, step

    def __mul__(self, n):
        return Idx(self.base * n, self.i, self.step * n)

    def __add__(self, n):
        return Idx(self.base + n, self.i, self.step)

    @property
    def val(self):
        return self.base if self.i is None else self.i * self.step + self.base

    def mod(self, m):
        assert self.i is None or self.step % m == 0
        return self.base % m

    def div(self, m):
        assert self.i is None or self.step % m == 0
        return Idx(self.base // m, self.i, self.step // m)


def steps(eng, lo, hi, body):
    n = (hi - lo) // 4
    if n > 1:
        with eng.Fori(0, n) as i:
            for k in range(4):
                body(Idx(lo + k, i, 4))
        lo += 4 * n
    for k in range(lo, hi):
        body(Idx(k))


class Phase:

    def __init__(self, name, kind, n, kt, src, raw0, own0):
        self.name, self.kind, self.n, self.kt, self.src = name, kind, n, kt, src
        self.raw0, self.own0 = raw0, own0





def trunk(nc, io):
    ctx = ExitStack()
    with ctx:
        def sem(name):
            return ctx.enter_context(nc.semaphore(name))

        top = [(nc.sbuf_base + 31) // 32 * 32]
        WORD = {F32: 4, F32R: 4, BF16: 2}

        def nbytes(shape, dt):
            n = WORD[dt]
            for x in shape[1:]:
                n *= x
            return (n + 31) // 32 * 32

        def put(name, shape, dt, at=None):
            where = top[0] if at is None else at
            if at is None:
                top[0] += nbytes(shape, dt)
                assert top[0] <= nc.sbuf_usable_end, (name, top[0])
            return nc.alloc_sbuf_tensor_at(name, list(shape), dt, offset=where)

        masks = put("masks", [P, len(MASKS), P], F32)
        level = put("level", [P, 2, LEVELS, P], BF16)
        vec = put("vec", [P, NVEC], F32)
        ada = put("ada", [P, 2, 48, 2], F32)
        raw = put("raw", [P, RAW, KT_DOWN * P], F32)
        xr = put("xr", [P, DT, TOK], F32)
        ZW = 2 * ADA_1 - 2
        scond = put("scond", [P, DT, 2 * ZW + 2], F32)
        ea = put("ea", [P, 1], F32)
        small = put("small", [P, 3 * TOK], F32)
        ss = put("ss", [P, NCH, 3, 4], F32)
        scratch0 = top[0]
        whi = put("whi", [P, SPL, KT_DOWN * P], F32R)
        wlo = put("wlo", [P, SPL, KT_DOWN * P], F32R)
        hhi_at = top[0]
        hhi = put("hhi", [P, DT, TOK], F32R)
        hlo = put("hlo", [P, DT, TOK], F32R)
        top_evac = top[0]
        evac = put("evac", [P, 8, TOK], F32)
        work0 = top[0]
        proj0 = nc.sbuf_usable_end // 32 * 32 - nbytes([P, 48, TOK], F32)
        rows_at = proj0 - nbytes([P, P + 3], F32)
        arow = put("arow", [P, P], F32, at=rows_at)
        pick = put("pick", [P, P + 3], F32, at=rows_at)
        proj = put("proj", [P, 48, TOK], F32, at=proj0)
        conv_out = proj[:, 0:CONV_T, :]
        gate = proj[:, CONV_T:48, :]
        yhi = put("yhi", [P, 16, TOK], F32R, at=proj0)
        ylo = put("ylo", [P, 16, TOK], F32R, at=proj0 + nbytes([P, 16, TOK], F32))
        ghi = put("ghi", [P, FF_T, TOK], F32R, at=proj0)
        glo = put("glo", [P, FF_T, TOK], F32R, at=proj0 + nbytes([P, FF_T, TOK], F32))
        sq = put("sq", [P, DT, TOK], F32, at=proj0)
        hmod = put("hmod", [P, DT, TOK], F32, at=proj0 + nbytes([P, DT, TOK], F32))
        assert work0 <= rows_at, (work0, rows_at)

        def mask(name):
            return masks[:, MASKS.index(name), :]

        def v(name):
            a, b = VEC[name]
            return vec[:, a:b]

        eps = v("eps")
        ident, ones = mask("ident"), mask("ones")
        cond = v("cond").rearrange("p (k c) -> p k c", c=2)
        ps = ctx.enter_context(nc.psum_tensor("ps", [P, 8, 512], F32))

        order, raw_n, own_n = [], 0, {"ada": 0, "split": 0}
        for name, kind, n, kt, src in (
                ("ada_first", "ada", ADA_1, KT_IN, io["w_ada"][0:ADA_1]),
                ("ssd_in", "split", N_IN, KT_IN, io["w_in"][0]),
                ("ada_rest", "ada", 2 * ADA_T - ADA_1, KT_IN, io["w_ada"][ADA_1:2 * ADA_T]),
                ("ssd_out", "split", N_OUT, KT_IN, io["w_out"][0]),
                ("up0", "split", 2 * FF_T, KT_IN, io["w_up"][0]), ("down0", "split", N_DOWN, KT_DOWN, io["w_down"][0]),
                ("gdn_in", "split", N_IN, KT_IN, io["w_in"][1]),
                ("gdn_out", "split", N_OUT, KT_IN, io["w_out"][1]),
                ("up1", "split", 2 * FF_T, KT_IN, io["w_up"][1]), ("down1", "split", N_DOWN, KT_DOWN, io["w_down"][1])):
            order.append(Phase(name, kind, n, kt, src, raw_n, own_n[kind]))
            raw_n += n
            own_n[kind] += n
        phase = {p.name: p for p in order}

        consts_in, x_in = sem("consts_in"), sem("x_in")
        raw_in = [sem(f"raw_in{s}") for s in range(RAW)]
        ada_used = sem("ada_used")
        hi_ready = sem("hi_ready")
        lo_ready = sem("lo_ready")
        blk_done = sem("blk_done")
        cond_zero, cond_silu = sem("cond_zero"), sem("cond_silu")
        ada_row, ada_tr = sem("ada_row"), sem("ada_tr")
        ada_ready = sem("ada_ready")
        h_mod, h_hi, h_lo = sem("h_mod"), sem("h_hi"), sem("h_lo")
        centre = sem("centre")
        left = sem("left")
        conv_done = sem("conv_done")
        conv_silu = sem("conv_silu")
        gate_done = sem("gate_done")
        gated = sem("gated")
        resid = sem("resid")
        f_centre = sem("f_centre")
        f_tap = sem("f_tap")
        up_out = sem("up_out")
        f_silu = sem("f_silu")
        g_hi, g_lo = sem("g_hi"), sem("g_lo")
        ln_mm, ln_mean, ln_cent, ln_sq, ln_std, ln_rstd, ln_norm, ln_x = (
            sem(x) for x in ("ln_mm", "ln_mean", "ln_cent", "ln_sq", "ln_std", "ln_rstd", "ln_norm", "ln_x"))
        y_scaled, y_hi, y_lo = sem("y_scaled"), sem("y_hi"), sem("y_lo")
        rms_sq, rms_mm, rms_std, rms_rstd = sem("rms_sq"), sem("rms_mm"), sem("rms_std"), sem("rms_rstd")
        dt_abs, dt_exp, dt_one, dt_ln, dt_rows, dt_tr, dt_tok, dt_cum, dt_dec, dt_last, dt_ch = (
            sem(x) for x in ("dt_abs", "dt_exp", "dt_one", "dt_ln", "dt_rows", "dt_tr", "dt_tok", "dt_cum", "dt_dec",
                             "dt_last", "dt_ch"))
        out_done = sem("out_done")

        def used(b):
            for p in order:
                if p.raw0 <= b < p.raw0 + p.n:
                    return (ada_used if p.kind == "ada" else lo_ready), p.own0 + b - p.raw0

        def load_block(sp, p, j):
            b = j + p.raw0
            if j.i is not None or j.base >= RAW:
                sp.wait_ge(ada_used if p.kind == "ada" else lo_ready, (j + (p.own0 - RAW + 1)).val)
            elif b.base >= RAW:
                s, count = used(b.base - RAW)
                sp.wait_ge(s, count + 1)
            sp.dma_start(raw[:, b.mod(RAW), 0:p.kt * P], p.src[j.val]).then_inc(raw_in[b.mod(RAW)], 16)

        def load_weights(sp, p):
            load_first(sp, p)
            load_rest(sp, p)

        def load_first(sp, p):
            for k in range(RAW):
                load_block(sp, p, Idx(k))

        def load_rest(sp, p):
            steps(sp, RAW, p.n, lambda j: load_block(sp, p, j))

        def split_hi(act, p, j):
            b, s = j + p.raw0, j + p.own0
            act.wait_ge(raw_in[b.mod(RAW)], ((b.div(RAW) + 1) * 16).val)
            act.wait_ge(blk_done, (s + 1).val)
            act.activation(whi[:, s.mod(SPL), 0:p.kt * P], raw[:, b.mod(RAW), 0:p.kt * P], ACT.Copy).then_inc(hi_ready, 1)

        def split_first(act, name):
            for k in range(2):
                split_hi(act, phase[name], Idx(k))

        def split_lo(pool, p, runs=()):
            def one(j):
                b, s = j + p.raw0, j + p.own0
                pool.wait_ge(hi_ready, (s + 1).val)
                pool.tensor_tensor(wlo[:, s.mod(SPL), 0:p.kt * P], raw[:, b.mod(RAW), 0:p.kt * P],
                                   whi[:, s.mod(SPL), 0:p.kt * P].bitcast(F32), ALU.subtract).then_inc(lo_ready, 1)
            in_runs(pool, 0, p.n, one, runs)

        def in_runs(eng, lo, hi, one, runs):
            for a, b, more in runs:
                if max(a, lo) >= min(b, hi):
                    continue
                steps(eng, lo, max(a, lo), one)

                def both(j, more=more):
                    one(j)
                    more(j)
                steps(eng, max(a, lo), min(b, hi), both)
                lo = min(b, hi)
            steps(eng, lo, hi, one)

        def multiply(pe, p, lo, hi, q, rhi, rlo, free, free0, banks, ready=None, runs=()):
            pe.sem_inc(free, banks)

            first_free = free0 + 1 - lo

            def one(j, ready=None):
                s, t, half = j + p.own0, j.div(q), j.base % q
                pe.wait_ge(lo_ready, (s + 1).val)
                if half == 0:
                    pe.wait_ge(free, (t + first_free).val)
                out = ps[:, t.mod(banks), 0:TOK]
                for k in range(p.kt):
                    a = whi[:, s.mod(SPL), k * P:(k + 1) * P]
                    b = wlo[:, s.mod(SPL), k * P:(k + 1) * P]
                    r = half * p.kt + k
                    if ready:
                        ready(r)
                    pe.matmul(out, a, rhi[:, r, :], start=(r == 0), stop=False)
                    pe.matmul(out, a, rlo[:, r, :], start=False, stop=False)
                    mm = pe.matmul(out, b, rhi[:, r, :], start=False, stop=(r == q * p.kt - 1))
                mm.then_inc(blk_done, 1)

            if ready:
                for k in range(q):
                    one(Idx(lo + k), ready)
                lo += q
            in_runs(pe, lo, hi, one, runs)

        def tile_done(eng, p, t, q=1):
            eng.wait_ge(blk_done, ((t + 1) * q + (p.own0 + SPL)).val)

        def staggered(eng, p, split, runs):
            for lo, hi, evacuate in runs:
                ahead = min(hi, p.n - 2)

                def both(s):
                    split(s + 2)
                    evacuate(s)
                if ahead > lo:
                    steps(eng, lo, ahead, both)
                for k in range(max(lo, ahead), hi):
                    evacuate(Idx(k))

        def busy(pe, bank, n):
            for k in range(n):
                pe.matmul(ps[:, bank, :], ident, masks[:, 1:5, :], start=True, stop=True)

        ada_flat = ada[:, :, :, :].rearrange("p l n c -> p (l n) c")

        def ada_block(pe, b, bank, k, n):
            pe.wait_ge(raw_in[b.mod(RAW)], ((b.div(RAW) + 1) * 16).val)
            for t in range(DT):
                mm = pe.matmul(ps[0:2 * n, bank, 0:P], scond[:, t, ZW - 2 * k:ZW - 2 * k + 2 * n],
                               raw[:, b.mod(RAW), t * P:(t + 1) * P],
                               start=(k == 0 and t == 0), stop=(k == n - 1 and t == DT - 1))
            mm.then_inc(ada_used, 1)

        def ada_columns(pe, n, bank):
            pe.matmul(ps[:, bank, 0:2 * n], arow[0:2 * n, :], ident[0:2 * n, 0:2 * n], start=True, stop=True).then_inc(ada_tr, 1)

        def ada_bias(dve, bank, first, n):
            return dve.tensor_tensor(ada_flat[:, bass.ds(first, n), :],
                                     ps[:, bank, 0:2 * n].rearrange("p (n c) -> p n c", c=2),
                                     v("b_ada")[:, bass.ds(first, n)].unsqueeze(2).to_broadcast([P, n, 2]), ALU.add)

        def ada_scale(dve, lay, part):
            w = ada[:, lay, part * DT:(part + 1) * DT, :]
            return dve.tensor_scalar(w, w, 1.0, None, ALU.add)

        def ada_first_pe(pe):
            pe.wait_ge(cond_silu, 1)
            for j in range(ADA_1):
                ada_block(pe, Idx(j), 5, j, ADA_1)
            pe.wait_ge(ada_row, 1)
            ada_columns(pe, ADA_1, 5)

        def ada_rows(act, bank, n):
            act.activation(arow[0:2 * n, :], ps[0:2 * n, bank, 0:P], ACT.Copy).then_inc(ada_row, 1)

        def ada_first_act(act):
            act.wait_ge(ada_used, ADA_1)
            ada_rows(act, 5, ADA_1)

        def ada_first_dve(dve):
            dve.wait_ge(ada_tr, 1)
            ada_bias(dve, 5, 0, ADA_1).then_inc(ada_ready, 1)
            dve.wait_ge(ada_ready, 1)
            ada_scale(dve, 0, 1).then_inc(ada_ready, 1)

        ADA_STEPS = 2 + SSD_G + 3
        SEQS = ((0, P, 0), (P, TOK, 1))

        def modulate_hi(act, m):
            lay, part = m // 2, 3 * (m % 2)
            act.wait_ge(ada_ready, ADA_STEPS if m else 2)
            for t in range(DT):
                act.wait_ge(ln_x, DT * (m - 1) + t + 1) if m else (act.wait_ge(x_in, 16) if t == 0 else None)
                for a, b, c in SEQS:
                    i = act.activation(hhi[:, t, a:b], xr[:, t, a:b], ACT.Identity,
                                       bias=ada[:, lay, part * DT + t, c:c + 1],
                                       scale=ada[:, lay, (part + 1) * DT + t, c:c + 1])
                i.then_inc(h_hi, 1)

        def modulate_lo(dve, m):
            lay, part = m // 2, 3 * (m % 2)
            dve.wait_ge(ada_ready, ADA_STEPS if m else 2)
            for t in range(DT):
                dve.wait_ge(ln_x, DT * (m - 1) + t + 1) if m else (dve.wait_ge(x_in, 16) if t == 0 else None)
                for a, b, c in SEQS:
                    i = dve.tensor_scalar(hmod[:, t, a:b], xr[:, t, a:b], ada[:, lay, (part + 1) * DT + t, c:c + 1],
                                          ada[:, lay, part * DT + t, c:c + 1], ALU.mult, ALU.add)
                i.then_inc(h_mod, 1)
                dve.wait_ge(h_mod, DT * m + t + 1)
                dve.wait_ge(h_hi, DT * m + t + 1)
                dve.tensor_tensor(hlo[:, t, :], hmod[:, t, :], hhi[:, t, :].bitcast(F32), ALU.subtract).then_inc(h_lo, 1)

        def h_ready(pe, m, k):
            pe.wait_ge(h_hi, DT * m + k + 1)
            pe.wait_ge(h_lo, DT * m + k + 1)

        def norm_sum(pe, n, t):
            first, last = (t.i is None and t.base == k for k in (0, DT - 1))
            pe.wait_ge(resid, (t + (2 + DT * n + 1)).val)
            mm = pe.matmul(ps[:, 6, 0:TOK], ones, xr[:, t.val, :], start=first, stop=last)
            if last:
                mm.then_inc(ln_mm, 1)

        def norm_pe(pe, n):
            norm_sum(pe, n, Idx(DT - 1))
            for t in range(DT):
                pe.wait_ge(ln_sq, DT * n + t + 1)
                mm = pe.matmul(ps[:, 7, 0:TOK], ones, sq[:, t, :], start=(t == 0), stop=(t == DT - 1))
            mm.then_inc(ln_mm, 1)

        def norm_dve(dve, n):
            lay, j = n // 2, n % 2
            mean, std, rstd = (small[:, k * TOK:(k + 1) * TOK] for k in range(3))
            g = v("ln_g").rearrange("p (n t) -> p n t", n=4)[:, n, :]
            b = v("ln_b").rearrange("p (n t) -> p n t", n=4)[:, n, :]
            dve.wait_ge(ln_mm, 2 * n + 1)
            dve.tensor_scalar(mean, ps[:, 6, 0:TOK], 1.0 / D, None, ALU.mult).then_inc(ln_mean, 1)
            dve.wait_ge(ln_mean, n + 1)
            for t in range(DT):
                dve.tensor_tensor(xr[:, t, :], xr[:, t, :], mean, ALU.subtract).then_inc(ln_cent, 1)
            dve.wait_ge(ln_std, n + 1)
            dve.reciprocal(rstd, std).then_inc(ln_rstd, 1)
            dve.wait_ge(ln_rstd, n + 1)
            for t in range(DT):
                dve.tensor_tensor(xr[:, t, :], xr[:, t, :], rstd, ALU.mult).then_inc(ln_norm, 1)
            for t in range(DT):
                dve.wait_ge(ln_norm, DT * n + t + 1)
                dve.tensor_scalar(xr[:, t, :], xr[:, t, :], g[:, t:t + 1], b[:, t:t + 1], ALU.mult, ALU.add).then_inc(ln_x, 1)

        def norm_act(act, n):
            std = small[:, TOK:2 * TOK]
            for t in range(DT):
                act.wait_ge(ln_cent, DT * n + t + 1)
                act.activation(sq[:, t, :], xr[:, t, :], ACT.Square).then_inc(ln_sq, 1)
            act.wait_ge(ln_mm, 2 * n + 2)
            act.activation(std, ps[:, 7, 0:TOK], ACT.Sqrt, scale=1.0 / D, bias=eps[:, 0:1]).then_inc(ln_std, 1)

        pick_set = sem("pick_set")
        l_sq, l_mm, l_std, l_inv, l_bc, l_done = (sem(x) for x in ("l_sq", "l_mm", "l_std", "l_inv", "l_bc", "l_done"))
        QK_T = 16
        L2_SQUARE, L2_SUM, L2_ROOT, L2_SPREAD = 17, 18, 34, 37
        inv = evac[:, 2:6, :]

        def l2_square(act, t):
            act.wait_ge(conv_silu, (t + (2 + CONV_T + 1)).val)
            act.wait_ge(l_mm, (t + 1).val)
            act.activation(evac[:, t.mod(2) + 6, :], proj[:, t.val, :], ACT.Square).then_inc(l_sq, 1)

        def l2_sum(pe, t):
            pe.wait_ge(l_sq, (t + 1).val)
            n = t.mod(4)
            pe.matmul(ps[:, (t.div(4) + 4).val, 0:TOK], pick[:, 3 - n:3 - n + P], evac[:, t.mod(2) + 6, :],
                      start=(n == 0), stop=(n == 3)).then_inc(l_mm, 1)

        def l2_root(act):
            act.wait_ge(l_mm, 2 + QK_T)
            act.activation(inv[:, 0:2, :], ps[:, 4:6, 0:TOK], ACT.Sqrt, scale=float(P), bias=eps[:, 2:3])
            act.activation(inv[:, 2:4, :], ps[:, 6:8, 0:TOK], ACT.Sqrt, bias=eps[:, 1:2]).then_inc(l_std, 1)

        def l2_spread(pe, j):
            for t in (j * 2, j * 2 + 1):
                pe.wait_ge(l_inv, (t.div(4) + 1).val)
                pe.wait_ge(l_done, (t + 1).val)
                pe.matmul(ps[:, 4 + t.mod(4), 0:TOK], ident[:, t.mod(4):t.mod(4) + 1].to_broadcast([P, P]),
                          evac[:, (t.div(4) + 2).val, :], start=True, stop=True).then_inc(l_bc, 1)

        def l2_scale(dve):
            dve.wait_ge(l_std, 1)
            for k in range(4):
                dve.reciprocal(inv[:, k, :], inv[:, k, :]).then_inc(l_inv, 1)

            def one(t):
                dve.wait_ge(l_bc, (t + 1).val)
                dve.tensor_tensor(proj[:, t.val, :], proj[:, t.val, :], ps[:, 4 + t.mod(4), 0:TOK], ALU.mult).then_inc(l_done, 1)
            steps(dve, 0, QK_T, one)

        def in_act(act, lay):
            p = phase[("ssd_in", "gdn_in")[lay]]
            cw = v("conv_w").rearrange("p (l t w) -> p l t w", l=2, w=3)[:, lay]
            cb = v("conv_b").rearrange("p (l t) -> p l t", l=2)[:, lay]

            def conv_centre(t):
                tile_done(act, p, t)
                act.wait_ge(conv_silu, (t + (32 * lay + 1)).val)
                act.activation(evac[:, t.mod(2), :], ps[:, t.mod(4), 0:TOK], ACT.Identity,
                               bias=cb[:, bass.ds(t.val, 1)], scale=cw[:, t.val, 1:2]).then_inc(centre, 1)

            def silu(t):
                act.wait_ge(conv_done, (t + (36 * lay + 4 + 1)).val)
                act.activation(proj[:, t.val, :], evac[:, t.mod(2), :], ACT.Silu).then_inc(conv_silu, 1)

            def conv_tile(t):
                conv_centre(t)
                silu(t + (-1))

            def gate_tile(t):
                tile_done(act, p, t)
                act.activation(proj[:, t.val, :], ps[:, t.mod(4), 0:TOK], ACT.Silu).then_inc(gate_done, 1)

            def first_gate(t):
                silu(t + (-1))
                gate_tile(t)

            if lay == 0:
                runs = [(0, 1, conv_centre), (1, 32, conv_tile), (32, 33, first_gate), (33, 48, gate_tile)]
            else:
                def squared(f):
                    def both(t):
                        f(t)
                        l2_square(act, t + (-L2_SQUARE))
                    return both

                def gate_root(t):
                    gate_tile(t)
                    l2_root(act)
                runs = [(0, 1, conv_centre), (1, L2_SQUARE, conv_tile), (L2_SQUARE, 32, squared(conv_tile)),
                        (32, 33, squared(first_gate)), (33, L2_ROOT, gate_tile), (L2_ROOT, L2_ROOT + 1, gate_root),
                        (L2_ROOT + 1, 48, gate_tile)]
            staggered(act, p, lambda j: split_hi(act, p, j), runs)

        def in_dve(dve, lay):
            cw = v("conv_w").rearrange("p (l t w) -> p l t w", l=2, w=3)[:, lay]

            def conv_taps(t):
                dve.wait_ge(centre, (t + (32 * lay + 1)).val)
                a, o = evac[:, t.mod(2), :], ps[:, t.mod(4), 0:TOK]
                for x, y in ((0, P), (P, TOK)):
                    i = dve.scalar_tensor_tensor(a[:, x + 1:y], o[:, x:y - 1], cw[:, t.val, 0:1], a[:, x + 1:y],
                                                 ALU.mult, ALU.add)
                i.then_inc(left, 1)
                dve.wait_ge(left, (t + (32 * lay + 1)).val)
                for x, y in ((0, P), (P, TOK)):
                    i = dve.scalar_tensor_tensor(a[:, x:y - 1], o[:, x + 1:y], cw[:, t.val, 2:3], a[:, x:y - 1],
                                                 ALU.mult, ALU.add)
                i.then_inc(conv_done, 1)
            if lay:
                dve.wait_ge(ada_tr, 1 + SSD_G)
                dve.memset(pick[:, 0:3], 0.0)
                dve.memset(pick[:, 4:P + 3], 0.0)
                dve.memset(pick[:, 3:4], 1.0).then_inc(pick_set, 1)
            steps(dve, 0, CONV_T, conv_taps)
            if lay:
                l2_scale(dve)

        def in_pe(pe, lay):
            p = phase[("ssd_in", "gdn_in")[lay]]
            norms = ((L2_SUM, L2_SUM + QK_T, lambda j: l2_sum(pe, j + (-L2_SUM))),
                     (L2_SPREAD, L2_SPREAD + QK_T // 2, lambda j: l2_spread(pe, j + (-L2_SPREAD)))) if lay else ()
            if lay:
                pe.sem_inc(l_mm, 2)
                pe.wait_ge(pick_set, 1)
            multiply(pe, p, 0, 32, 1, hhi, hlo, conv_done, 36 * lay, 4, lambda k: h_ready(pe, 2 * lay, k), norms)
            pe.wait_ge(conv_done, 36 * (lay + 1))
            multiply(pe, p, 32, 49, 1, hhi, hlo, gate_done, 20 * lay, 4, None, norms)

        def back_pe(pe, name, n, rhi, rlo, ready):
            p = phase[name]

            def sums(j):
                if j.base % 2:
                    norm_sum(pe, n, (j + (-3)).div(2))
            multiply(pe, p, 0, p.n, 2, rhi, rlo, gated, 10 * n, 2, ready, ((2, 4, sums), (4, p.n, sums)))

        def back_act(act, name, n):
            p, lay, part = phase[name], n // 2, 2 + 3 * (n % 2)

            def gate_out(j):
                if j.base % 2 == 0:
                    return
                t = j.div(2)
                tile_done(act, p, t, 2)
                act.wait_ge(resid, (t + (8 * n + 1)).val)
                for a, b, c in SEQS:
                    i = act.activation(evac[:, t.mod(2), a:b], ps[:, t.mod(2), a:b], ACT.Identity,
                                       scale=ada[:, lay, bass.ds((t + part * DT).val, 1), c])
                i.then_inc(gated, 1)
            act.wait_ge(ada_ready, ADA_STEPS)
            staggered(act, p, lambda j: split_hi(act, p, j), [(0, p.n, gate_out)])

        def back_dve(dve, n):
            def add(t):
                dve.wait_ge(gated, (t + (10 * n + 2 + 1)).val)
                dve.scalar_tensor_tensor(xr[:, t.val, :], xr[:, t.val, :], ALPHA, evac[:, t.mod(2), :],
                                         ALU.mult, ALU.add).then_inc(resid, 1)
            steps(dve, 0, DT, add)

        def up_pe(pe, lay):
            multiply(pe, phase[f"up{lay}"], 0, 2 * FF_T, 1, hhi, hlo, up_out, 48 * lay, 4,
                     lambda k: h_ready(pe, 2 * lay + 1, k))

        def up_act(act, lay):
            p = phase[f"up{lay}"]
            fw = v("ffn_w").rearrange("p (l t w) -> p l t w", l=2, w=9)[:, lay]
            fb = v("ffn_b").rearrange("p (l t) -> p l t", l=2)[:, lay]

            def tile_centre(j):
                t = j.div(2)
                tile_done(act, p, j)
                act.wait_ge(f_silu, (t + (FF_T * lay + 1)).val)
                act.activation(evac[:, t.mod(2), :], ps[:, j.mod(4), 0:TOK], ACT.Identity,
                               bias=fb[:, bass.ds(t.val, 1)], scale=fw[:, t.val, 4:5]).then_inc(f_centre, 1)

            def hidden_hi(t):
                act.wait_ge(up_out, (t * 2 + (48 * lay + 4 + 2)).val)
                act.activation(ghi[:, t.val, :], evac[:, t.mod(2) + 4, :], ACT.Copy).then_inc(g_hi, 1)

            def silu(j):
                t = j.div(2)
                act.wait_ge(up_out, (t * 2 + (48 * lay + 4 + 1)).val)
                act.activation(evac[:, t.mod(2) + 2, :], evac[:, t.mod(2), :], ACT.Silu).then_inc(f_silu, 1)

            def evacuate(j):
                if j.base % 2:
                    silu(j)
                else:
                    tile_centre(j)
                    hidden_hi(j.div(2) + (-1))
            staggered(act, p, lambda j: split_hi(act, p, j), [(0, 1, tile_centre), (1, 2, silu), (2, p.n, evacuate)])
            hidden_hi(Idx(FF_T - 1))

        def up_dve(dve, lay):
            p = phase[f"up{lay}"]
            fw = v("ffn_w").rearrange("p (l t w) -> p l t w", l=2, w=9)[:, lay]
            taps = [(0, -1, 0), (0, -1, 1), (0, 1, 0), (0, 1, 1)] + [(r, c, 0) for r in (-1, 1) for c in (0, -1, 1)]
            behind = [None, None, 0, 1] + list(range(2, 3)) + list(range(4, 9))

            def all_taps(j):
                t = j.div(2)
                dve.wait_ge(f_centre, (t + (FF_T * lay + 1)).val)
                a, o = evac[:, t.mod(2), :], ps[:, j.mod(4), 0:TOK]
                for n, (r, c, prompt) in enumerate(taps):
                    w = fw[:, t.val, (r + 1) * 3 + c + 1:(r + 1) * 3 + c + 2]
                    c0, c1 = max(0, -c), max(0, c)
                    if prompt:
                        x, y = a[:, c0:P - c1], o[:, c0 + c:P - c1 + c]
                    else:
                        grid_a = a[:, P:TOK].rearrange("p (r c) -> p r c", c=GRID_W)
                        grid_o = o[:, P:TOK].rearrange("p (r c) -> p r c", c=GRID_W)
                        r0, r1 = max(0, -r), GRID_H - max(0, r)
                        x = grid_a[:, r0:r1, c0:GRID_W - c1]
                        y = grid_o[:, r0 + r:r1 + r, c0 + c:GRID_W - c1 + c]
                    if behind[n] is not None:
                        dve.wait_ge(f_tap, (t * 9 + (9 * FF_T * lay + behind[n] + 1)).val)
                    i = dve.scalar_tensor_tensor(x, y, w, x, ALU.mult, ALU.add)
                    i.then_inc(f_tap if n < len(taps) - 1 else up_out, 1)

            def hidden_lo(t):
                dve.wait_ge(g_hi, (t + (FF_T * lay + 2 + 1)).val)
                dve.tensor_tensor(glo[:, t.val, :], evac[:, t.mod(2) + 4, :], ghi[:, t.val, :].bitcast(F32),
                                  ALU.subtract).then_inc(g_lo, 1)

            def product(j):
                t = j.div(2)
                dve.wait_ge(f_silu, (t + (FF_T * lay + 3)).val)
                tile_done(dve, p, j)
                dve.wait_ge(g_hi, (t + (FF_T * lay + 1)).val)
                dve.tensor_tensor(evac[:, t.mod(2) + 4, :], ps[:, j.mod(4), 0:TOK], evac[:, t.mod(2) + 2, :],
                                  ALU.mult).then_inc(up_out, 1)

            def evacuate(j):
                if j.base % 2:
                    product(j)
                else:
                    all_taps(j)
                    hidden_lo(j.div(2) + (-1))
            all_taps(Idx(0))
            product(Idx(1))
            steps(dve, 2, 2 * FF_T, evacuate)
            hidden_lo(Idx(FF_T - 1))
        rows = put("rows", [P, 8, TOK], F32, at=hhi_at)
        NH = (SSD_H, GDN_H)
        NB = tuple(6 * n for n in NH)
        tok_s = small[:, 0:2 * NCH * 64].rearrange("p (k c n) -> p k c n", k=2, c=NCH)
        tok_g = small[:, 0:NCH * 64].rearrange("p (c n) -> p c n", c=NCH)
        dec_s = small[:, 384:384 + NCH * NB[0]].rearrange("p (c n) -> p c n", c=NCH)
        dec_g = small[:, 384:384 + NCH * NB[1]].rearrange("p (c n) -> p c n", c=NCH)
        wdt = small[:, 960:1152].rearrange("p (c n) -> p c n", c=NCH)
        bec = small[:, 960:960 + NCH * 32].rearrange("p (c n) -> p c n", c=NCH)
        DT_CH = 9

        def decay_act(act, lay):
            act.wait_ge(dt_abs, lay + 1)
            act.activation(rows[0:64, 2, :], rows[0:64, 1, :], ACT.Exp)
            act.activation(ea[0:64, :], v("a_log")[0:64, lay:lay + 1], ACT.Exp)
            act.activation(rows[32:64, 6, :], rows[32:64, 0, :], ACT.Exp, scale=-1.0).then_inc(dt_exp, 1)
            act.wait_ge(dt_one, lay + 1)
            act.activation(rows[0:64, 4, :], rows[0:64, 3, :], ACT.Ln).then_inc(dt_ln, 1)
            act.wait_ge(dt_cum, lay + 1)
            dec = (dec_s, dec_g)[lay]
            for c in range(NCH):
                i = act.activation(dec[:, c, :], ps[:, 6 + c // 2, (c % 2) * NB[lay]:(c % 2 + 1) * NB[lay]], ACT.Exp)
            i.then_inc(dt_dec, 1)

        def decay_dve(dve, lay):
            r = [rows[0:64, k, :] for k in range(8)]
            n = [DT_CH * lay]

            def chain(ins):
                n[0] += 1
                ins.then_inc(dt_ch, 1)
                dve.wait_ge(dt_ch, n[0])

            tile_done(dve, phase[("ssd_in", "gdn_in")[lay]], Idx(48))
            chain(dve.tensor_scalar(r[0], ps[0:64, 0, 0:TOK], v("dt_bias")[0:64, lay:lay + 1], None, ALU.add))
            dve.scalar_tensor_tensor(r[1], r[0], -1.0, r[0], ALU.mult, ALU.min).then_inc(dt_abs, 1)
            dve.wait_ge(dt_exp, lay + 1)
            dve.tensor_scalar(r[3], r[2], 1.0, None, ALU.add).then_inc(dt_one, 1)
            dve.wait_ge(dt_one, lay + 1)
            chain(dve.tensor_scalar(r[5], r[3], -1.0, None, ALU.add))
            chain(dve.tensor_scalar(r[7], r[5], 0.0, None, ALU.is_equal))
            chain(dve.tensor_tensor(r[5], r[5], r[7], ALU.add))
            chain(dve.reciprocal(r[5], r[5]))
            dve.wait_ge(dt_ln, lay + 1)
            chain(dve.tensor_tensor(r[4], r[4], r[7], ALU.add))
            chain(dve.tensor_tensor(r[4], r[4], r[2], ALU.mult))
            chain(dve.tensor_tensor(r[4], r[4], r[5], ALU.mult))
            chain(dve.scalar_tensor_tensor(r[7], r[0], 0.0, r[4], ALU.max, ALU.add))
            if lay == 0:
                dve.tensor_scalar(r[1], r[7], ea[0:64, :], -1.0, ALU.mult, ALU.mult).then_inc(dt_rows, 1)
            else:
                dve.tensor_scalar(rows[0:32, 1, :], rows[0:32, 7, :], ea[0:32, :], -1.0, ALU.mult, ALU.mult)
                dve.tensor_scalar(rows[32:64, 2, :], rows[32:64, 6, :], 1.0, None, ALU.add).then_inc(dt_one, 1)
                dve.wait_ge(dt_one, lay + 2)
                dve.reciprocal(rows[32:64, 1, :], rows[32:64, 2, :]).then_inc(dt_rows, 1)
            dve.wait_ge(dt_tr, lay + 1)
            w = (2 if lay == 0 else 1) * NCH * 64
            dve.tensor_copy(small[:, 0:w], ps[:, 1, 0:w]).then_inc(dt_tok, 1)
            dve.wait_ge(dt_dec, lay + 1)
            if lay == 0:
                dve.tensor_tensor(wdt, dec_s[:, :, 64:128], tok_s[:, 0], ALU.mult).then_inc(dt_last, 1)
            else:
                dve.tensor_tensor(bec, dec_g[:, :, 0:32], tok_g[:, :, 32:64], ALU.mult).then_inc(dt_last, 1)

        def decay_pe(pe, lay):
            pe.wait_ge(dt_rows, lay + 1)
            for k in range(2 if lay == 0 else 1):
                for c in range(NCH):
                    r = rows[0:64, (7, 1)[k] if lay == 0 else 1, c * P:(c + 1) * P]
                    mm = pe.transpose(ps[:, 1, (k * NCH + c) * 64:(k * NCH + c + 1) * 64], r, ident[0:64, 0:64])
            mm.then_inc(dt_tr, 1)
            pe.wait_ge(dt_tok, lay + 1)
            h = NH[lay]
            for c in range(NCH):
                a = tok_s[:, 1, c, :] if lay == 0 else tok_g[:, c, 0:32]
                o = ps[:, 6 + c // 2, (c % 2) * NB[lay]:(c % 2 + 1) * NB[lay]]
                for k, (m, lo, hi) in enumerate((("le", 0, h), ("ge", h, 2 * h), ("gt", 0, h), ("lt", h, 2 * h))):
                    pe.matmul(o[:, k * h:(k + 1) * h], mask(m), a[:, lo:hi], start=True, stop=True)
                mm = pe.matmul(o[:, 4 * h:6 * h], ones, a[:, 0:2 * h], start=True, stop=True)
            mm.then_inc(dt_cum, 1)

        st = [scratch0]

        def tmp(name, shape, dt=F32):
            t = put(name, shape, dt, at=st[0])
            st[0] += nbytes([P] + list(shape[1:]), dt)
            assert st[0] <= proj0, (name, st[0], proj0)
            return t

        stg = tmp("stg", [P, 2, 4, TOK])
        s0 = tmp("s0", [P, 2, 2, 256])
        xtok = tmp("xtok", [P, 2, NCH, TOK])
        seg_r = tmp("seg_r", [P, 2, 2, 512])
        e_s = tmp("e_s", [P, 2, 512])
        ge_s = tmp("ge_s", [P, 2, 2, 512])
        gm_s = tmp("gm_s", [P, NCH, 2, P])
        xw = tmp("xw", [P, 2, 4, 256])
        sdec = tmp("sdec", [P, 2, 2, 256])
        s1 = tmp("s1", [P, 2, 2, 256])
        xdt = tmp("xdt", [P, 2, 2, 256])
        inter = tmp("inter", [P, 512])
        ytok = tmp("ytok", [P, 2, 256])
        vtmp = tmp("vtmp", [P, 2, 2, P])
        st_sb = tmp("st_sb", [P, 2, 512])
        ADA_G = (2 * ADA_T - ADA_1) // SSD_G
        assert st[0] <= rows_at
        s_stg = [sem(f"s_stg{k}") for k in range(2)]
        s_out = [sem(f"s_out{k}") for k in range(2)]
        (s_a, s_xtok, s_gm, s_r, s_seg, s_exp, s_ge, s_xw, s_st, s_dec, s_new, s_stout, s_xdt, s_mm, s_yc, s_y,
         s_yt, s_vt, s_v) = (sem(x) for x in (
             "s_a", "s_xtok", "s_gm", "s_r", "s_seg", "s_exp", "s_ge", "s_xw", "s_st", "s_dec", "s_new", "s_stout",
             "s_xdt", "s_mm", "s_yc", "s_y", "s_yt", "s_vt", "s_v"))
        s_it = sem("s_it")

        def groups(eng, body):
            with eng.Fori(0, SSD_G // 2) as i:
                for b in range(2):
                    body(Idx(b, i, 2), lambda c, b=b, i=i: Idx(3 * b + c, i, 6), b)

        def tokens(c):
            return slice(c * P, (c + 1) * P)

        def heads(ap, n):
            return ap.unsqueeze(2).to_broadcast([P, 4, n])

        def h4(ap):
            return ap.rearrange("p (h n) -> p h n", h=4)

        def stage(eng, g, b):
            gg = g.val % SSD_G
            eng.dma_start(stg[:, b, 0:2, :], proj[:, bass.ds(gg * 2, 2), :]).then_inc(s_stg[b], 16)
            eng.dma_start(stg[:, b, 2, :], proj[:, gg + 16, :]).then_inc(s_stg[b], 16)
            eng.dma_start(stg[:, b, 3, :], proj[:, gg + 24, :]).then_inc(s_stg[b], 16)
            eng.dma_start(s0[:, b, :, :], io["s_ssd"][gg]).then_inc(s_stg[b], 16)

        def ssd_sp(sp):
            p = phase["ada_rest"]
            sp.wait_ge(lo_ready, phase["ssd_in"].n)

            def group(g, u, b):
                def block(n):
                    load_block(sp, p, Idx(ADA_G * b + n, g.i, 2 * ADA_G))
                for n in range(4):
                    block(n)
                if b == 0:
                    sp.wait_ge(conv_silu, 2 + CONV_T)
                    sp.wait_ge(blk_done, phase["ssd_in"].own0 + N_IN + SPL)
                    sp.wait_ge(dt_last, 1)
                sp.wait_ge(s_v, (u(0) + 2).val)
                stage(sp, g + 1, 1 - b)
                block(4)
                block(5)
                sp.wait_ge(s_stout, (g + 1).val)
                sp.dma_start(io["o_ssd"][g.val], st_sb[:, b, :].rearrange("p (d n) -> p d n", d=2)).then_inc(s_out[b], 16)
                for n in range(6, ADA_G):
                    block(n)
            groups(sp, group)

        def ssd_act(act):
            act.wait_ge(conv_silu, 2 + CONV_T)
            act.wait_ge(blk_done, phase["ssd_in"].own0 + N_IN + SPL)
            act.wait_ge(dt_dec, 1)
            act.wait_ge(dt_last, 1)
            stage(act, Idx(0), 0)

            def group(g, u, b):
                act.wait_ge(s_stg[b], (g.div(2) * 64 + 64).val)
                for c in range(NCH):
                    act.wait_ge(s_a, (u(c) + 1).val)
                    act.wait_ge(s_xdt, (u(c) + 1).val)
                    act.wait_ge(s_st, (u(c) + 1).val)
                    act.activation(xtok[:, b, c, :], ps[:, c, 0:TOK], ACT.Copy).then_inc(s_xtok, 1)
                act.wait_ge(s_st, (u(0) + 7).val)
                act.wait_ge(s_out[b], (g.div(2) * 16 + 16).val)
                act.activation(st_sb[:, b, :], ps[:, 7, :], ACT.Copy).then_inc(s_stout, 1)
                for c in range(NCH):
                    act.wait_ge(s_seg, (u(c) + 3).val)
                    act.wait_ge(s_ge, (u(c) + 1).val)
                    act.activation(e_s[:, u(c).mod(2), :], ps[:, 3, :], ACT.Exp).then_inc(s_exp, 1)
                act.wait_ge(ada_used, (g * ADA_G + (ADA_1 + ADA_G)).val)
                act.wait_ge(ada_tr, (g + 1).val)
                ada_rows(act, 0, ADA_G)
            groups(act, group)
            for b in range(2):
                act.wait_ge(s_stg[b], 64 * (SSD_G // 2 + 1 - b))
                act.wait_ge(s_out[b], 16 * (SSD_G // 2 + 1))
            act.wait_ge(s_v, 2 + 3 * SSD_G)

        def ssd_pool(pool):
            pool.wait_ge(dt_last, 1)
            pool.wait_ge(blk_done, phase["ssd_in"].own0 + N_IN + SPL)

            def group(g, u, b):
                def dt_a(c, d):
                    return tok_s[:, 1, c, bass.ds((g * 4 + 32 * d).val, 4)]

                def segments(c):
                    pool.wait_ge(s_seg, (u(c) + 1).val)
                    m = ("le", "ge")
                    for d in range(2):
                        i = pool.tensor_tensor(h4(seg_r[:, u(c).mod(2), d, :]),
                                               mask(m[d]).unsqueeze(1).to_broadcast([P, 4, P]), heads(dt_a(c, d), P), ALU.mult)
                    i.then_inc(s_r, 1)

                def x_dt(c):
                    pool.wait_ge(s_xtok, (u(c) + 4).val)
                    pool.wait_ge(s_mm, (u(c) + 1).val)
                    for d in range(2):
                        i = pool.tensor_tensor(h4(xdt[:, u(c).mod(2), d, :]), h4(xtok[:, b, c, 0:256]),
                                               heads(tok_s[:, 0, c, bass.ds((g * 4 + 32 * d).val, 4)], SSD_P), ALU.mult)
                    i.then_inc(s_xdt, 1)

                def weighted(c, d, k):
                    return pool.tensor_tensor(h4(xw[:, b, k, :]), h4(xtok[:, b, c, 0:256]),
                                              heads(wdt[:, c, bass.ds((g * 4 + 32 * d).val, 4)], SSD_P), ALU.mult)

                segments(0)
                for c in range(NCH):
                    pool.wait_ge(s_xtok, (u(c) + 4).val)
                    pool.wait_ge(s_st, (u(c) + 1).val)
                    if c == CTX:
                        weighted(c, 0, 0)
                    i = weighted(c, (1, 0, 1)[c], c + 1)
                    i.then_inc(s_xw, 1)
                pool.wait_ge(s_stg[b], (g.div(2) * 64 + 64).val)
                for d in range(2):
                    pool.wait_ge(s_new, (g * 2 + (d + 1)).val)
                    pool.tensor_tensor(h4(sdec[:, b, d, :]), h4(s0[:, b, d, :]),
                                       heads(dec_s[:, 1 + d, bass.ds((g * 4 + (128 + 32 * d)).val, 4)], SSD_P),
                                       ALU.mult).then_inc(s_dec, 1)
                x_dt(0)
                segments(1)
                x_dt(1)
                segments(2)
                x_dt(2)
            groups(pool, group)

        def ssd_pe(pe):
            for s, n in ((s_seg, 2), (s_mm, 2), (s_st, 6), (s_yt, 2)):
                pe.sem_inc(s, n)

            def group(g, u, b):
                pe.wait_ge(s_stg[b], (g.div(2) * 64 + 64).val)
                for c in range(NCH):
                    pe.wait_ge(s_xtok, (u(c) + 1).val)
                    pe.wait_ge(s_gm, (u(c) + 1).val)
                    for k in range(3):
                        pe.transpose(ps[:, c, k * P:(k + 1) * P], stg[:, b, k, tokens(c)], ident)
                    pe.matmul(ps[:, c, 3 * P:4 * P], stg[:, b, 2, tokens(c)], stg[:, b, 3, tokens(c)],
                              start=True, stop=True).then_inc(s_a, 1)

                def segment(c):
                    pe.wait_ge(s_exp, (u(c) + 1).val)
                    pe.wait_ge(s_r, (u(c) + 1).val)
                    r = seg_r[:, u(c).mod(2)]
                    pe.matmul(ps[:, 3, :], mask("gt"), r[:, 0, :], start=True, stop=False)
                    pe.matmul(ps[:, 3, :], mask("lt"), r[:, 1, :], start=False, stop=True).then_inc(s_seg, 1)

                def outputs(c):
                    y = 5 + u(c).mod(2)
                    pe.wait_ge(s_v, (u(c) + 1).val)
                    pe.wait_ge(s_yc, (u(c) + 1).val)
                    pe.wait_ge(s_ge, (u(c) + 3).val)
                    pe.wait_ge(s_xdt, (u(c) + 7).val)
                    if c != CTX:
                        pe.wait_ge(s_new, (g * 2 + 6).val)
                        f, w = (s0[:, b, 0, :], s1[:, b, 1, :]) if c == LAT1 else (s1[:, b, 0, :], s0[:, b, 1, :])
                        pe.matmul(ps[:, 4, 0:256], stg[:, b, 3, tokens(c)], f, start=True, stop=True)
                        pe.matmul(ps[:, 4, 256:512], stg[:, b, 3, tokens(c)], w, start=True, stop=True)
                    for h in range(4):
                        for d in range(2):
                            mm = pe.matmul(ps[:, y, h * SSD_P:(h + 1) * SSD_P], ge_s[:, u(c).mod(2), d, h * P:(h + 1) * P],
                                           xdt[:, u(c).mod(2), d, h * SSD_P:(h + 1) * SSD_P], start=(d == 0), stop=(d == 1))
                    mm.then_inc(s_mm, 1)

                def back(c):
                    pe.wait_ge(s_y, (u(c) + 1).val)
                    for k in range(2):
                        i = pe.transpose(ps[:, 5 + u(c).mod(2), 256 + k * P:256 + (k + 1) * P],
                                         ytok[:, u(c).mod(2), k * P:(k + 1) * P], ident)
                    i.then_inc(s_yt, 1)

                def ada_blocks(lo, hi):
                    if lo == 0:
                        pe.wait_ge(s_gm, (u(0) + 4).val)
                    for n in range(lo, hi):
                        ada_block(pe, Idx(ada0 + ADA_G * b + n, g.i, 2 * ADA_G), 0, n, ADA_G)
                ada0 = phase["ada_rest"].raw0
                pe.wait_ge(ada_ready, (g + 2).val)
                segment(0)
                ada_blocks(0, 3)
                for c in range(NCH):
                    pe.wait_ge(s_xw, (u(c) + 1).val)
                    if c == CTX:
                        pe.wait_ge(s_new, (g * 2 + 4).val)
                    if c == LAT1:
                        pe.wait_ge(s_stout, (g + 1).val)
                    for d, k in (((0, 0), (1, 1)), ((0, 2),), ((1, 3),))[c]:
                        mm = pe.matmul(ps[:, 7, d * 256:(d + 1) * 256], xtok[:, b, c, 256:384], xw[:, b, k, :],
                                       start=True, stop=True)
                    mm.then_inc(s_st, 1)
                ada_blocks(3, 5)
                segment(1)
                outputs(0)
                ada_blocks(5, 6)
                segment(2)
                outputs(1)
                ada_blocks(6, 8)
                back(0)
                outputs(2)
                ada_blocks(8, 10)
                back(1)
                back(2)
                pe.wait_ge(ada_row, (g + 2).val)
                pe.wait_ge(s_exp, (u(2) + 2).val)
                ada_columns(pe, ADA_G, 3)
            groups(pe, group)

        def ssd_dve(dve):
            zg, dskip = gate, v("d_skip")

            def group(g, u, b):
                for c in range(NCH):
                    dve.wait_ge(s_xtok, (u(c) + 4).val)
                    for d, m in enumerate(("le", "ge")):
                        i = dve.tensor_tensor(gm_s[:, c, d, :], ps[:, c, 3 * P:4 * P], mask(m), ALU.mult)
                    i.then_inc(s_gm, 1)

                def decayed(c):
                    dve.wait_ge(s_exp, (u(c) + 2).val)
                    dve.wait_ge(s_mm, (u(c) + 1).val)
                    dve.wait_ge(s_gm, (u(c) + 4).val)
                    for d in range(2):
                        i = dve.tensor_tensor(h4(ge_s[:, u(c).mod(2), d, :]), h4(e_s[:, u(c).mod(2), :]),
                                              gm_s[:, c, d, :].unsqueeze(1).to_broadcast([P, 4, P]), ALU.mult)
                    i.then_inc(s_ge, 1)

                def combine(c):
                    k = u(c).mod(2)
                    dve.wait_ge(s_mm, (u(c) + 3).val)
                    dve.wait_ge(s_yt, (u(c) + 1).val)
                    y = ps[:, 5 + k, 0:256]
                    if c == CTX:
                        dve.tensor_copy(ytok[:, k, :], y).then_inc(s_y, 1)
                        dve.sem_inc(s_yc, 1)
                        return
                    dve.wait_ge(s_y, u(c).val)
                    for d in range(2):
                        i = dve.tensor_tensor(h4(inter[:, d * 256:(d + 1) * 256]), h4(ps[:, 4, d * 256:(d + 1) * 256]),
                                              heads(dec_s[:, c, bass.ds((g * 4 + 32 * d).val, 4)], SSD_P), ALU.mult)
                    i.then_inc(s_yc, 1)
                    dve.wait_ge(s_yc, (u(c) + 2).val)
                    dve.tensor_tensor(inter[:, 0:256], inter[:, 0:256], inter[:, 256:512], ALU.add).then_inc(s_it, 1)
                    dve.wait_ge(s_it, (g * 2 + c).val)
                    dve.tensor_tensor(ytok[:, k, :], y, inter[:, 0:256], ALU.add).then_inc(s_y, 1)

                def gated_out(c):
                    dve.wait_ge(s_yt, (u(c) + 3).val)
                    dve.wait_ge(s_v, (u(c) + 1).val)
                    for k in range(2):
                        i = dve.scalar_tensor_tensor(vtmp[:, u(c).mod(2), k, :], stg[:, b, k, tokens(c)], dskip[:, bass.ds((g * 2 + k).val, 1)],
                                                     ps[:, 5 + u(c).mod(2), 256 + k * P:256 + (k + 1) * P], ALU.mult, ALU.add)
                    i.then_inc(s_vt, 1)
                    dve.wait_ge(s_vt, (u(c) + 1).val)
                    z = zg[:, bass.ds((g * 2).val, 2), tokens(c)]
                    dve.tensor_tensor(z, z, vtmp[:, u(c).mod(2)], ALU.mult).then_inc(s_v, 1)

                dve.wait_ge(s_st, (u(2) + 7).val)
                for d in range(2):
                    dve.wait_ge(s_dec, (g * 2 + (d + 1)).val)
                    dve.tensor_tensor(s1[:, b, d, :], sdec[:, b, d, :], ps[:, 7, d * 256:(d + 1) * 256],
                                      ALU.add).then_inc(s_new, 1)
                decayed(0)
                decayed(1)
                combine(0)
                decayed(2)
                combine(1)
                gated_out(0)
                combine(2)
                gated_out(1)
                gated_out(2)
                dve.wait_ge(ada_tr, (g + 2).val)
                ada_bias(dve, 3, (g * ADA_G + ADA_1).val, ADA_G).then_inc(ada_ready, 1)
            dve.wait_ge(gate_done, 20)
            groups(dve, group)
            dve.wait_ge(ada_ready, 2 + SSD_G)
            for lay, part in ((0, 4), (1, 1), (1, 4)):
                ada_scale(dve, lay, part).then_inc(ada_ready, 1)

        def rms_act(act):
            std = small[:, 0:TOK]

            def square(t):
                act.wait_ge(rms_mm, (t + 1).val)
                act.activation(evac[:, t.mod(2) + 6, :], gate[:, t.val, :], ACT.Square).then_inc(rms_sq, 1)
            steps(act, 0, 16, square)
            act.wait_ge(rms_mm, 2 + 16)
            act.activation(std, ps[:, 7, 0:TOK], ACT.Sqrt, scale=1.0 / 2048, bias=eps[:, 1:2]).then_inc(rms_std, 1)

        def rms_pe(pe):
            pe.sem_inc(rms_mm, 2)
            for t in range(16):
                pe.wait_ge(rms_sq, t + 1)
                pe.matmul(ps[:, 7, 0:TOK], ones, evac[:, t % 2 + 6, :], start=(t == 0), stop=(t == 15)).then_inc(rms_mm, 1)

        def mixer_hi(act, lay):
            def one(t):
                if lay == 0:
                    act.wait_ge(y_scaled, (t + 1).val)
                act.activation(yhi[:, t.val, :], gate[:, t.val, :], ACT.Copy).then_inc(y_hi, 1)
            steps(act, 0, 16, one)

        def mixer_lo(dve, lay):
            rstd = small[:, TOK:2 * TOK]
            nw = v("ssd_norm")
            if lay == 0:
                dve.wait_ge(rms_std, 1)
                dve.reciprocal(rstd, small[:, 0:TOK]).then_inc(rms_rstd, 1)
                dve.wait_ge(rms_rstd, 1)

            def one(t):
                if lay == 0:
                    dve.scalar_tensor_tensor(gate[:, t.val, :], gate[:, t.val, :], nw[:, bass.ds(t.val, 1)], rstd,
                                             ALU.mult, ALU.mult).then_inc(y_scaled, 1)

            def two(t):
                dve.wait_ge(y_hi, (t + (16 * lay + 1)).val)
                dve.tensor_tensor(ylo[:, t.val, :], gate[:, t.val, :], yhi[:, t.val, :].bitcast(F32),
                                  ALU.subtract).then_inc(y_lo, 1)
            for k in (0, 8):
                if lay == 0:
                    steps(dve, k, k + 8, one)
                steps(dve, k, k + 8, two)

        def y_ready(pe, lay, k):
            pe.wait_ge(y_hi, 16 * lay + k + 1)
            pe.wait_ge(y_lo, 16 * lay + k + 1)
        st[0] = scratch0
        stq = tmp("stq", [P, 4, TOK])
        U = tmp("U", [P, NCH, 8, P])
        T_at = st[0]
        T = tmp("T", [P, NCH, 8, P])
        N_at = st[0]
        N = tmp("N", [P, NCH, 8, P])
        O_at = st[0]
        Noff = tmp("Noff", [P, NCH, 8, P])
        V_at = st[0]
        V = tmp("V", [P, NCH, 8, P])
        qk = tmp("qk", [P, NCH, 2, 512])
        vtok = tmp("vtok", [P, NCH, 512])
        vtok_at = st[0] - nbytes([P, NCH, 512], F32)
        stv = put("stv", [P, 4, TOK], F32, at=O_at)
        gr = [put(f"gr{c}", [P, 2, 512], F32, at=(V_at, T_at, T_at + 4096)[c]) for c in range(NCH)]
        ge = [put(f"ge{c}", [P, 512], F32, at=(V_at + 4096, T_at + 8192, T_at + 10240)[c]) for c in range(NCH)]
        gke = put("gke", [P, 512], F32, at=V_at + 6144)
        gkq = put("gkq", [P, 2, 256], F32, at=V_at + 8192)
        rhs = put("rhs", [P, 4, 512], F32, at=T_at)
        ktok = put("ktok", [P, NCH, 256], F32, at=T_at + 8192)
        bv = put("bv", [P, 6, 512], F32, at=N_at)
        vn = put("vn", [P, 6, 512], F32, at=O_at)
        S0 = put("S0", [P, 2, 512], F32, at=V_at)
        S1 = put("S1", [P, 2, 512], F32, at=V_at + 4096)
        vd = put("vd", [P, 2, 512], F32, at=V_at + 8192)
        ot = put("ot", [P, 3, 512], F32, at=vtok_at)
        (g_r, g_kkq, g_kk, g_seg, g_e, g_et, g_vt, g_vtok, g_ke, g_n, g_qk, g_off, g_w1, g_u0, g_t0, g_rst, g_v1, g_ut,
         g_u, g_t, g_bv, g_kt, g_ktok, g_tr, g_ks, g_rr, g_vn, g_vd, g_st, g_sd, g_s1, g_so, g_om, g_ss, g_rs, g_on,
         g_yt, g_v, g_c, g_sum, g_sq, g_stg, g_s0, g_sout, lev_in, lev_ready) = (sem(x) for x in (
             "g_r g_kkq g_kk g_seg g_e g_et g_vt g_vtok g_ke g_n g_qk g_off g_w1 g_u0 g_t0 g_rst g_v1 g_ut g_u g_t g_bv "
             "g_kt g_ktok g_tr g_ks g_rr g_vn g_vd g_st g_sd g_s1 g_so g_om g_ss g_rs g_on g_yt g_v g_c g_sum g_sq g_stg g_s0 "
             "g_sout lev_in lev_ready").split())
        lev32 = put("lev32", [P, 2, LEVELS, P], F32, at=top_evac)
        HG = GDN_H // 4
        TASKS = ((CTX, 0), (CTX, 1), (LAT1, 0), (LAT2, 1), (LAT2, 0), (LAT1, 1))
        SLOT = (2, 3, 0, 1, 0, 1)

        def turns(eng, body):
            with eng.Fori(0, HG) as i:
                body(i, lambda k, n: Idx(k, i, n))

        class Chain:

            def __init__(self, eng, s, i, per_turn):
                self.eng, self.s, self.i, self.per, self.n = eng, s, i, per_turn, 0

            def __call__(self, ins):
                self.n += 1
                ins.then_inc(self.s, 1)
                self.eng.wait_ge(self.s, self.i * self.per + self.n)

            def end(self):
                assert self.n == self.per, self.n

        def heads4(ap, n=P):
            return ap.unsqueeze(2).to_broadcast([P, 4, n])

        def col(t, c, first, d, i):
            return t[:, c, bass.ds(i * 4 + (first + GDN_H * d), 4)]

        def half(ap, l, odd):
            return ap.rearrange("p n (b t s) -> p n b t s", t=2, s=1 << l)[:, :, :, odd, :]

        def half1(ap, l, odd):
            return ap.rearrange("p (b t s) -> p b t s", t=2, s=1 << l)[:, :, odd, :]

        def packed(ap, l):
            return ap.rearrange("p (n b s) -> p n b s", n=4, s=1 << l)

        def gdn_sp(sp):
            sp.wait_ge(dt_last, 2)
            sp.wait_ge(l_done, 4 + QK_T)
            sp.wait_ge(gate_done, 40)

            def turn(i, at):
                sp.wait_ge(g_om, at(1, 3).val)
                sp.wait_ge(g_sout, at(16, 32).val)
                sp.dma_start(stq[:, 0:2, :], proj[:, bass.ds(i * 2 + 8, 2), :]).then_inc(g_stg, 16)
                sp.dma_start(stq[:, 2:4, :], proj[:, bass.ds(i * 2, 2), :]).then_inc(g_stg, 16)
                sp.dma_start(stv[:, :, :], proj[:, bass.ds(i * 4 + 16, 4), :]).then_inc(g_stg, 16)
                sp.wait_ge(g_ut, at(18, 18).val)
                sp.dma_start(S0[:, :, :], io["s_gdn"][i]).then_inc(g_s0, 16)
                for q in range(2):
                    sp.wait_ge(g_so, at(q + 1, 2).val)
                    sp.dma_start(io["o_gdn"][i][:, q, :], rhs[:, SLOT[q], :]).then_inc(g_sout, 16)
            turns(sp, turn)

        def gdn_act(act):
            act.wait_ge(dt_last, 2)
            act.wait_ge(l_done, 4 + QK_T)
            act.wait_ge(gate_done, 40)

            def turn(i, at):
                act.wait_ge(g_v, at(1, 3).val)
                for c in range(NCH):
                    u = at(c, 3)
                    act.wait_ge(g_seg, (u + 2).val)
                    act.activation(ge[c][:, :], ps[:, 2 * c, :], ACT.Exp).then_inc(g_e, 1)
                    act.wait_ge(g_vt, (u + 1).val)
                    act.activation(vtok[:, c, :], ps[:, 2 * c + 1, :], ACT.Copy).then_inc(g_vtok, 1)
                for l in range(1, LEVELS):
                    for c in range(NCH):
                        act.wait_ge(g_ut, at(3 * (l - 1) + c + 1, 18).val)
                        for d in range(2):
                            a = act.activation(half(U[:, c, 4 * d:4 * d + 4, :], l, 1 - d),
                                               packed(ps[:, 2 * c + 1, 256 * d:256 * d + 256], l), ACT.Copy)
                        a.then_inc(g_u, 1)
                        if l < LEVELS - 1:
                            for d in range(2):
                                a = act.activation(half(T[:, c, 4 * d:4 * d + 4, :], l, d),
                                                   packed(ps[:, 2 * c, 256 * d:256 * d + 256], l), ACT.Copy)
                            a.then_inc(g_t, 1)
                act.wait_ge(g_kt, at(1, 2).val)
                act.activation(ktok[:, 0:2, :], ps[:, 6, :].rearrange("p (c n) -> p c n", c=2), ACT.Copy)
                act.wait_ge(g_kt, at(2, 2).val)
                act.activation(ktok[:, 2, :], ps[:, 7, 0:256], ACT.Copy).then_inc(g_ktok, 1)

                def solved(q):
                    act.wait_ge(g_tr, at(q + 1, 6).val)
                    act.activation(vn[:, q, :], ps[:, (0, 1, 4, 5, 4, 5)[q], :], ACT.Copy).then_inc(g_vn, 1)

                def state_out(q):
                    act.wait_ge(g_st, at(q + 1, 4).val)
                    act.activation(rhs[:, SLOT[q], :], ps[:, 6 + q, :], ACT.Copy).then_inc(g_so, 1)
                for q in range(4):
                    solved(q)
                for q in range(2):
                    state_out(q)
                solved(4)
                solved(5)
            turns(act, turn)
            act.wait_ge(g_v, 1 + 3 * HG)
            act.wait_ge(g_sout, 16 + 32 * HG)

        def gdn_pool(pool):
            pool.wait_ge(lev_ready, 1)

            def turn(i, at):
                pool.wait_ge(g_stg, at(48, 48).val)
                pool.wait_ge(g_vn, at(1, 6).val)
                for c in range(NCH):
                    for d, m in enumerate(("gt", "lt")):
                        a = pool.tensor_tensor(h4(gr[c][:, d, :]), mask(m).unsqueeze(1).to_broadcast([P, 4, P]),
                                               heads4(col(tok_g, c, 0, d, i)), ALU.mult)
                    a.then_inc(g_r, 1)

                def off(l, c):
                    for d in range(2):
                        a = pool.tensor_tensor(Noff[:, c, 4 * d:4 * d + 4, :], N[:, c, 4 * d:4 * d + 4, :],
                                               level[:, d, l, :].unsqueeze(1).to_broadcast([P, 4, P]), ALU.mult)
                    a.then_inc(g_off, 1)
                for c in range(NCH):
                    pool.wait_ge(g_vt, at(3, 3).val)
                    pool.wait_ge(g_n, at(c + 2, 3).val)
                    off(0, c)
                for l in range(1, LEVELS):
                    for c in range(NCH):
                        pool.wait_ge(g_w1, at(3 * (l - 1) + c + 1, 21).val)
                        if l == 1:
                            pool.wait_ge(g_t0, at(c + 1, 3).val)
                        off(l, c)
                pool.wait_ge(g_off, at(21, 21).val)
                for q, (c, d) in enumerate(TASKS):
                    pool.wait_ge(g_vtok, at(c + 1, 3).val)
                    pool.tensor_tensor(h4(bv[:, q, :]), h4(vtok[:, c, :]), heads4(col(tok_g, c, 32, d, i)),
                                       ALU.mult).then_inc(g_bv, 1)
                pool.wait_ge(g_s0, at(16, 16).val)
                for d in range(2):
                    pool.tensor_tensor(h4(S1[:, d, :]), h4(S0[:, d, :]), heads4(col(dec_g, 1 + d, 64, d, i)),
                                       ALU.mult).then_inc(g_sd, 1)
                for c in range(NCH):
                    pool.wait_ge(g_ss, at(c + 1, 3).val)
                    pool.tensor_tensor(ss[:, c, 2, :], ss[:, c, 1, :], eps[:, 3:4].to_broadcast([P, 4]), ALU.pow).then_inc(g_rs, 1)
            turns(pool, turn)

        def gdn_pe(pe):
            for s, n in ((g_seg, 1), (g_et, 1), (g_om, 1)):
                pe.sem_inc(s, n)

            def turn(i, at):
                pe.wait_ge(g_stg, at(48, 48).val)
                pe.wait_ge(g_v, at(1, 3).val)

                def products(c):
                    tk = tokens(c)
                    pe.wait_ge(g_kk, at(c + 1, 3).val)
                    for k in range(2):
                        mm = pe.matmul(ps[:, 6, k * 256:(k + 1) * 256].rearrange("p (t n) -> p t n", t=2),
                                       stq[:, k, tk], stq[:, k:k + 3:2, tk], start=True, stop=True)
                    mm.then_inc(g_kkq, 1)

                def segments(c):
                    pe.wait_ge(g_r, at(c + 1, 3).val)
                    pe.matmul(ps[:, 2 * c, :], mask("le"), gr[c][:, 0, :], start=True, stop=False)
                    pe.matmul(ps[:, 2 * c, :], mask("ge"), gr[c][:, 1, :], start=False, stop=True).then_inc(g_seg, 1)
                    for h in range(4):
                        mm = pe.transpose(ps[:, 2 * c + 1, h * P:(h + 1) * P], stv[:, h, tokens(c)], ident)
                    mm.then_inc(g_vt, 1)

                def turned(c):
                    pe.wait_ge(g_e, at(c + 2, 3).val)
                    for h in range(4):
                        mm = pe.transpose(ps[:, 2 * c, h * P:(h + 1) * P], ge[c][:, h * P:(h + 1) * P], ident)
                    mm.then_inc(g_et, 1)
                products(0)
                segments(0)
                segments(1)
                turned(0)
                products(1)
                segments(2)
                turned(1)
                products(2)
                turned(2)
                for c in range(NCH):
                    pe.wait_ge(g_off, at(c + 1, 21).val)
                    pe.wait_ge(g_qk, at(c + 1, 3).val)
                    pe.wait_ge(g_vtok, at(c + 1, 3).val)
                    for n in range(8):
                        mm = pe.transpose(ps[:, 2 * c + n // 4, (n % 4) * P:(n % 4 + 1) * P], Noff[:, c, n, :], ident)
                    mm.then_inc(g_w1, 1)
                for l in range(1, LEVELS):
                    for c in range(NCH):
                        pe.wait_ge(g_off, at(3 * l + c + 1, 21).val)
                        if l == 1:
                            pe.wait_ge(g_u0, at(c + 1, 3).val)
                            if c == 0:
                                busy(pe, 6, 5)
                        else:
                            pe.wait_ge(g_u, at(3 * (l - 2) + c + 1, 18).val)
                            pe.wait_ge(g_t, at(3 * (l - 2) + c + 1, 15).val)
                        for n in range(8):
                            d = n // 4
                            mm = pe.matmul(ps[:, 2 * c, n * 64:(n + 1) * 64], Noff[:, c, n, :], half1(U[:, c, n, :], l, 1 - d),
                                           start=True, stop=True)
                        mm.then_inc(g_w1, 1)
                    for c in range(NCH):
                        pe.wait_ge(g_v1, at(3 * (l - 1) + c + 1, 18).val)
                        if l == 1:
                            pe.wait_ge(g_t0, at(c + 1, 3).val)
                        for n in range(8):
                            d = n // 4
                            mm = pe.matmul(ps[:, 2 * c + 1, n * 64:(n + 1) * 64], T[:, c, n, :], half1(V[:, c, n, :], l, 1 - d),
                                           start=True, stop=True)
                        if l < LEVELS - 1:
                            for n in range(8):
                                d = n // 4
                                mm = pe.matmul(ps[:, 2 * c, n * 64:(n + 1) * 64], V[:, c, n, :], half1(T[:, c, n, :], l, d),
                                               start=True, stop=True)
                        mm.then_inc(g_ut, 1)
                for c in range(NCH):
                    for k in range(2):
                        mm = pe.transpose(ps[:, 6 + c // 2, (c % 2) * 256 + k * P:(c % 2) * 256 + (k + 1) * P],
                                          stq[:, k, tokens(c)], ident)
                    if c:
                        mm.then_inc(g_kt, 1)

                def solve(q, r):
                    c, d = TASKS[q]
                    for h in range(4):
                        mm = pe.matmul(ps[:, (0, 1, 4, 5, 4, 5)[q], h * P:(h + 1) * P], U[:, c, 4 * d + h, :],
                                       r[:, h * P:(h + 1) * P], start=True, stop=True)
                    mm.then_inc(g_tr, 1)

                def state_read(q, s):
                    c, d = TASKS[q]
                    for k in range(2):
                        mm = pe.matmul(ps[:, 2 + d, k * 256:(k + 1) * 256], stq[:, k, tokens(c)], s[:, k * 256:(k + 1) * 256],
                                       start=True, stop=True)
                    mm.then_inc(g_ks, 1)

                def state_add(q):
                    c, d = TASKS[q]
                    pe.wait_ge(g_vd, at(q + 1, 4).val)
                    for k in range(2):
                        mm = pe.matmul(ps[:, 6 + d, k * 256:(k + 1) * 256], ktok[:, c, k * P:(k + 1) * P],
                                       vd[:, q % 2, k * 256:(k + 1) * 256], start=True, stop=True)
                    mm.then_inc(g_st, 1)

                def outputs(c):
                    b = (0, 1, 4)[c]
                    if c != CTX:
                        pe.wait_ge(g_s1, at(2, 2).val)
                        f, w = (S0[:, 0], S1[:, 1]) if c == LAT1 else (S1[:, 0], S0[:, 1])
                        for k in range(2):
                            for bank, s in ((b + 1, f), (b + 2, w)):
                                pe.matmul(ps[:, bank, k * 256:(k + 1) * 256], stq[:, 2 + k, tokens(c)],
                                          s[:, k * 256:(k + 1) * 256], start=True, stop=True)
                    for h in range(4):
                        for d in range(2):
                            q = TASKS.index((c, d))
                            mm = pe.matmul(ps[:, b, h * P:(h + 1) * P], qk[:, c, d, h * P:(h + 1) * P],
                                           vn[:, q, h * P:(h + 1) * P], start=(d == 0), stop=(d == 1))
                    mm.then_inc(g_om, 1)

                def back(c):
                    pe.wait_ge(g_on, at(c + 1, 3).val)
                    pe.wait_ge(g_v, at(c + 1, 3).val)
                    for h in range(4):
                        mm = pe.transpose(ps[:, 7, h * P:(h + 1) * P], ot[:, 2, h * P:(h + 1) * P], ident)
                    mm.then_inc(g_yt, 1)

                pe.wait_ge(g_u, at(18, 18).val)
                for q in range(2):
                    pe.wait_ge(g_bv, at(q + 1, 6).val)
                    solve(q, bv[:, q])
                pe.wait_ge(g_s0, at(16, 16).val)
                for q in (2, 3):
                    state_read(q, S0[:, TASKS[q][1]])
                for q in (2, 3):
                    pe.wait_ge(g_rr, at(q - 1, 4).val)
                    solve(q, rhs[:, SLOT[q]])
                pe.wait_ge(g_ktok, at(1, 1).val)
                state_add(0)
                state_add(1)
                for q in (2, 3):
                    pe.wait_ge(g_so, at(q - 1, 2).val)
                    state_add(q)
                outputs(CTX)
                for q in (4, 5):
                    pe.wait_ge(g_s1, at(TASKS[q][1] + 1, 2).val)
                    state_read(q, S1[:, TASKS[q][1]])
                for q in (4, 5):
                    pe.wait_ge(g_rr, at(q - 1, 4).val)
                    pe.wait_ge(g_vn, at(q, 6).val)
                    solve(q, rhs[:, SLOT[q]])
                back(CTX)
                pe.wait_ge(g_vn, at(7, 6).val)
                outputs(LAT1)
                outputs(LAT2)
                busy(pe, 0, 3)
                back(LAT1)
                busy(pe, 0, 6)
                back(LAT2)
            turns(pe, turn)

        def gdn_dve(dve):
            nw = v("gdn_norm")

            def turn(i, at):
                chain = Chain(dve, g_c, i, 11)

                def kpair(t):
                    return ps[:, 6, :].rearrange("p (k t n) -> p k t n", k=2, t=2)[:, :, t, :]

                for c in range(NCH):
                    u = at(c, 3)
                    dve.wait_ge(g_kkq, (u + 1).val)
                    dve.wait_ge(g_e, (u + 2).val)
                    dve.wait_ge(g_n, (u + 1).val)
                    dve.tensor_tensor(gke[:, :].rearrange("p (k r n) -> p k r n", k=2, r=2),
                                      kpair(0).unsqueeze(2).to_broadcast([P, 2, 2, P]),
                                      ge[c][:, :].rearrange("p (k r n) -> p k r n", k=2, r=2), ALU.mult).then_inc(g_ke, 1)
                    dve.wait_ge(g_qk, at(c, 3).val) if c else None
                    for d, m in enumerate(("le", "ge")):
                        a = dve.tensor_tensor(gkq[:, d, :].rearrange("p (k n) -> p k n", k=2), kpair(1),
                                              mask(m).unsqueeze(1).to_broadcast([P, 2, P]), ALU.mult)
                    a.then_inc(g_kk, 1)
                    dve.wait_ge(g_ke, (u + 1).val)
                    for d in range(2):
                        a = dve.scalar_tensor_tensor(N[:, c, 4 * d:4 * d + 4, :], h4(gke[:, :]), -1.0,
                                                     heads4(col(tok_g, c, 32, d, i)), ALU.mult, ALU.mult)
                    a.then_inc(g_n, 1)
                    dve.wait_ge(g_et, (u + 2).val)
                    dve.wait_ge(g_kk, (u + 2).val)
                    for d in range(2):
                        a = dve.tensor_tensor(qk[:, c, d, :].rearrange("p (k r n) -> p k r n", k=2, r=2),
                                              ps[:, 2 * c, :].rearrange("p (k r n) -> p k r n", k=2, r=2),
                                              gkq[:, d, :].rearrange("p (k n) -> p k n", k=2).unsqueeze(2)
                                              .to_broadcast([P, 2, 2, P]), ALU.mult)
                    a.then_inc(g_qk, 1)
                for c in range(NCH):
                    dve.wait_ge(g_off, at(c + 1, 21).val)
                    for d in range(2):
                        a = dve.tensor_tensor(T[:, c, 4 * d:4 * d + 4, :], Noff[:, c, 4 * d:4 * d + 4, :],
                                              ident.unsqueeze(1).to_broadcast([P, 4, P]), ALU.add)
                    a.then_inc(g_t0, 1)
                    dve.wait_ge(g_w1, at(c + 1, 21).val)
                    for d in range(2):
                        a = dve.tensor_tensor(U[:, c, 4 * d:4 * d + 4, :], h4(ps[:, 2 * c + d, :]),
                                              ident.unsqueeze(1).to_broadcast([P, 4, P]), ALU.add)
                    a.then_inc(g_u0, 1)
                for l in range(1, LEVELS):
                    for c in range(NCH):
                        if l == 1:
                            dve.wait_ge(g_n, at(4, 3).val)
                            dve.wait_ge(g_qk, at(3, 3).val)
                        else:
                            dve.wait_ge(g_ut, at(3 * (l - 2) + c + 1, 18).val)
                        for d in range(2):
                            a = dve.tensor_copy(half(V[:, c, 4 * d:4 * d + 4, :], l, d),
                                                half1(ident, l, d).unsqueeze(1).to_broadcast([P, 4, 64 >> l, 1 << l]))
                        a.then_inc(g_rst, 1)
                        dve.wait_ge(g_w1, at(3 * l + c + 1, 21).val)
                        for d in range(2):
                            a = dve.tensor_tensor(half(V[:, c, 4 * d:4 * d + 4, :], l, 1 - d),
                                                  packed(ps[:, 2 * c, 256 * d:256 * d + 256], l),
                                                  half1(ident, l, 1 - d).unsqueeze(1).to_broadcast([P, 4, 64 >> l, 1 << l]),
                                                  ALU.add)
                        a.then_inc(g_v1, 1)

                def right_side(q):
                    c, d = TASKS[q]
                    dve.wait_ge(g_ks, at(q - 1, 4).val)
                    dve.wait_ge(g_bv, at(q + 1, 6).val)
                    r = rhs[:, SLOT[q], :]
                    if q >= 4:
                        dve.wait_ge(g_tr, at(q - 1, 6).val)
                    chain(dve.tensor_tensor(h4(r), h4(ps[:, 2 + d, :]), heads4(col(bec, c, 0, d, i)), ALU.mult))
                    dve.tensor_tensor(r, bv[:, q, :], r, ALU.subtract).then_inc(g_rr, 1)

                def decayed(q):
                    c, d = TASKS[q]
                    dve.wait_ge(g_vn, at(q + 2, 6).val)
                    if q >= 2:
                        dve.wait_ge(g_st, at(q - 1, 4).val)
                    dve.tensor_tensor(h4(vd[:, q % 2, :]), h4(vn[:, q, :]), heads4(col(dec_g, c, 32, d, i)),
                                      ALU.mult).then_inc(g_vd, 1)

                def total(c):
                    b = (0, 1, 4)[c]
                    o, t = ot[:, 0, :], ot[:, 1, :]
                    dve.wait_ge(g_om, at(c + 2, 3).val)
                    if c == CTX:
                        dve.wait_ge(g_bv, at(6, 6).val)
                        chain(dve.tensor_copy(o, ps[:, b, :]))
                    else:
                        dve.wait_ge(g_on, at(c, 3).val)
                        dve.tensor_tensor(h4(o), h4(ps[:, b + 1, :]), heads4(col(dec_g, c, 0, 0, i)), ALU.mult)
                        chain(dve.tensor_tensor(h4(t), h4(ps[:, b + 2, :]), heads4(col(dec_g, c, 0, 1, i)), ALU.mult))
                        chain(dve.tensor_tensor(o, o, t, ALU.add))
                        chain(dve.tensor_tensor(o, o, ps[:, b, :], ALU.add))
                    dve.tensor_tensor(t, o, o, ALU.mult).then_inc(g_sq, 1)
                    dve.wait_ge(g_sq, at(c + 1, 3).val)
                    dve.tensor_reduce(ss[:, c, 0, :], h4(t), AX_X, ALU.add).then_inc(g_sum, 1)
                    dve.wait_ge(g_sum, at(c + 1, 3).val)
                    dve.tensor_scalar(ss[:, c, 1, :], ss[:, c, 0, :], 1.0 / P, RMS_EPS, ALU.mult, ALU.add).then_inc(g_ss, 1)

                def normed(c):
                    dve.wait_ge(g_rs, at(c + 1, 3).val)
                    if c:
                        dve.wait_ge(g_yt, at(c, 3).val)
                    dve.tensor_tensor(h4(ot[:, 2, :]), h4(ot[:, 0, :]), heads4(ss[:, c, 2, :]), ALU.mult).then_inc(g_on, 1)

                def gated_out(c):
                    dve.wait_ge(g_yt, at(c + 1, 3).val)
                    z = gate[:, bass.ds(i * 4, 4), tokens(c)]
                    dve.scalar_tensor_tensor(z, h4(ps[:, 7, :]), nw[:, 0:1], z, ALU.mult, ALU.mult).then_inc(g_v, 1)

                right_side(2)
                right_side(3)
                for q in range(4):
                    decayed(q)
                for d in range(2):
                    dve.wait_ge(g_st, at(3 + d, 4).val)
                    dve.wait_ge(g_sd, at(d + 1, 2).val)
                    dve.tensor_tensor(S1[:, d, :], S1[:, d, :], ps[:, 6 + d, :], ALU.add).then_inc(g_s1, 1)
                total(CTX)
                right_side(4)
                right_side(5)
                normed(CTX)
                gated_out(CTX)
                total(LAT1)
                normed(LAT1)
                total(LAT2)
                gated_out(LAT1)
                normed(LAT2)
                gated_out(LAT2)
                chain.end()
            turns(dve, turn)
        block = ctx.enter_context(nc.Block())

        @block.sync
        def _(sp):
            sp.dma_start(vec[:], io["vec"]).then_inc(consts_in, 16)
            sp.dma_start(masks[:], io["masks"]).then_inc(consts_in, 16)
            sp.dma_start(lev32[:], io["level"]).then_inc(lev_in, 16)
            sp.dma_start(xr[:], io["x"]).then_inc(x_in, 16)
            for name in ("ada_first", "ssd_in"):
                load_weights(sp, phase[name])
            ssd_sp(sp)
            for name in ("ssd_out", "up0", "down0", "gdn_in"):
                load_weights(sp, phase[name])
            load_first(sp, phase["gdn_out"])
            gdn_sp(sp)
            load_rest(sp, phase["gdn_out"])
            for name in ("up1", "down1"):
                load_weights(sp, phase[name])
            sp.wait_ge(ln_x, 2 * DEPTH * DT)
            sp.dma_start(io["y"], xr[:]).then_inc(out_done, 16)
            sp.wait_ge(out_done, 16)
            for b in range(2):
                sp.wait_ge(s_out[b], 16 * (SSD_G // 2 + 1))

        @block.gpsimd
        def _(pool):
            for lay in range(DEPTH):
                split_lo(pool, phase[("ssd_in", "gdn_in")[lay]])
                (ssd_pool, gdn_pool)[lay](pool)
                for name in (("ssd_out", "gdn_out")[lay], f"up{lay}", f"down{lay}"):
                    split_lo(pool, phase[name])

        @block.scalar
        def _(act):
            act.sem_inc(g_hi, 2)
            for s, n in ((s_xtok, 3), (s_exp, 1), (conv_silu, 2), (f_silu, 2), (g_e, 1), (g_vn, 1),
                         (g_sout, 16)):
                act.sem_inc(s, n)
            act.wait_ge(consts_in, 32)
            act.wait_ge(lev_in, 16)
            act.activation(level[:], lev32[:], ACT.Copy).then_inc(lev_ready, 1)
            act.wait_ge(cond_zero, 1)
            act.activation(scond[:, :, ZW:ZW + 2], cond, ACT.Silu).then_inc(cond_silu, 1)
            ada_first_act(act)
            for lay in range(DEPTH):
                if lay == 0:
                    split_first(act, "ssd_in")
                modulate_hi(act, 2 * lay)
                in_act(act, lay)
                decay_act(act, lay)
                if lay == 0:
                    ssd_act(act)
                    split_first(act, "ssd_out")
                    rms_act(act)
                else:
                    gdn_act(act)
                    split_first(act, "gdn_out")
                mixer_hi(act, lay)
                back_act(act, ("ssd_out", "gdn_out")[lay], 2 * lay)
                split_first(act, f"up{lay}")
                norm_act(act, 2 * lay)
                modulate_hi(act, 2 * lay + 1)
                up_act(act, lay)
                split_first(act, f"down{lay}")
                back_act(act, f"down{lay}", 2 * lay + 1)
                if lay == 0:
                    split_first(act, "gdn_in")
                norm_act(act, 2 * lay + 1)

        @block.tensor
        def _(pe):
            pe.sem_inc(blk_done, SPL)
            pe.wait_ge(consts_in, 32)
            for lay in range(DEPTH):
                if lay == 0:
                    ada_first_pe(pe)
                in_pe(pe, lay)
                decay_pe(pe, lay)
                if lay == 0:
                    ssd_pe(pe)
                    rms_pe(pe)
                else:
                    gdn_pe(pe)
                back_pe(pe, ("ssd_out", "gdn_out")[lay], 2 * lay, yhi, ylo, lambda k: y_ready(pe, lay, k))
                norm_pe(pe, 2 * lay)
                up_pe(pe, lay)

                def hidden_ready(k):
                    pe.wait_ge(g_hi, 2 + FF_T * lay + k + 1)
                    pe.wait_ge(g_lo, FF_T * lay + k + 1)
                back_pe(pe, f"down{lay}", 2 * lay + 1, ghi, glo, hidden_ready)
                norm_pe(pe, 2 * lay + 1)

        @block.vector
        def _(dve):
            dve.memset(scond[:, :, :], 0.0).then_inc(cond_zero, 1)
            for s, n in ((resid, 2), (s_gm, 3), (s_ge, 2), (s_xdt, 6), (s_new, 4), (s_yc, 1), (s_v, 2),
                         (s_out[0], 16), (s_out[1], 16),
                         (l_done, 4), (g_kk, 1), (g_n, 1), (g_v, 1)):
                dve.sem_inc(s, n)
            dve.wait_ge(consts_in, 32)
            for lay in range(DEPTH):
                if lay == 0:
                    ada_first_dve(dve)
                modulate_lo(dve, 2 * lay)
                in_dve(dve, lay)
                decay_dve(dve, lay)
                if lay == 0:
                    ssd_dve(dve)
                else:
                    gdn_dve(dve)
                mixer_lo(dve, lay)
                back_dve(dve, 2 * lay)
                norm_dve(dve, 2 * lay)
                modulate_lo(dve, 2 * lay + 1)
                up_dve(dve, lay)
                back_dve(dve, 2 * lay + 1)
                norm_dve(dve, 2 * lay + 1)


def layouts(q):
    import numpy as np
    f = {k: np.asarray(a) for k, a in q.items()}

    def cols(a):
        a = a.reshape(a.shape[:-1] + (-1, P))
        return np.moveaxis(a, -1, 0)

    def blocks(w, kt, q):
        w = np.pad(w, ((0, 0), (0, -w.shape[1] % P)))
        m = w.shape[1] // P
        w = w.reshape(q, kt, P, m, P)
        return np.ascontiguousarray(w.transpose(3, 0, 2, 1, 4)).reshape(m * q, P, kt * P)

    vec = np.zeros((P, NVEC), np.float32)

    def fill(name, a):
        lo, hi = VEC[name]
        a = a.reshape(a.shape[0], -1)
        vec[:a.shape[0], lo:hi] = a
    fill("b_ada", cols(f["b_ada"]))
    fill("ln_g", cols(f["ln_g"]))
    fill("ln_b", cols(f["ln_b"]))
    cw = np.stack([f["ssd_conv_w"][0], f["gdn_conv_w"][0]])
    fill("conv_w", cols(cw).transpose(0, 1, 3, 2))
    cb = np.zeros((2, CONV_T * P), np.float32)
    cb[0] = f["ssd_conv_b"][0]
    fill("conv_b", cols(cb))
    for name, s, g in (("dt_bias", "ssd_dt_bias", "gdn_dt_bias"), ("a_log", "ssd_a_log", "gdn_a_log")):
        a = np.zeros((P, 2), np.float32)
        a[:64, 0] = f[s].reshape(-1)
        a[:32, 1] = f[g].reshape(-1)
        fill(name, a)
    fill("d_skip", cols(np.repeat(f["ssd_d"][0], SSD_P)))
    fill("ssd_norm", cols(f["ssd_norm_w"][0]))
    fill("gdn_norm", f["gdn_norm_w"][0].reshape(P, 1))
    fill("ffn_w", cols(f["ffn_conv_w"]).transpose(0, 1, 4, 2, 3))
    fill("ffn_b", cols(f["ffn_conv_b"]))
    fill("cond", cols(np.stack([f["c_ctx"], f["c"][0]])).transpose(0, 2, 1))
    vec[:, VEC["eps"][0]:VEC["eps"][1]] = np.array([LN_EPS, RMS_EPS, P * RMS_EPS, -0.5], np.float32)

    p, n = np.arange(P)[:, None], np.arange(P)[None, :]
    masks = np.stack([p == n, p <= n, p >= n, p > n, p < n, p >= 0 * n], 1).astype(np.float32)
    lev = np.zeros((P, 2, LEVELS, P), np.float32)
    for l in range(LEVELS):
        s = 1 << l
        pair, odd = (p >> (l + 1)) == (n >> (l + 1)), ((p // s) % 2 == 1) & ((n // s) % 2 == 0)
        lev[:, 0, l] = pair & odd
        lev[:, 1, l] = (pair & odd).T
    x = np.concatenate([f["x_prompt"][0], f["x_sample"][0]], 0)

    sin, gin = f["ssd_w_in"][0], f["gdn_w_in"][0]
    sin = np.concatenate([sin[:, 2048:6144], sin[:, :2048], sin[:, 6144:]], 1)
    up = []
    for w in f["ffn_w_up"]:
        a = blocks(w, KT_IN, 1)
        up.append(np.stack([a[:FF_T], a[FF_T:]], 1).reshape(2 * FF_T, P, KT_IN * P))
    s_ssd = np.stack([f["state_ssd_fwd"][0, 0], f["state_ssd_bwd"][0, 0]])
    s_ssd = s_ssd.reshape(2, SSD_G, 256, P).transpose(1, 3, 0, 2)
    s_gdn = np.stack([f["state_gdn_fwd"][0, 0], f["state_gdn_bwd"][0, 0]])
    s_gdn = s_gdn.reshape(2, 4, 4, P, P).transpose(1, 3, 0, 2, 4)
    out = {
        "vec": vec, "masks": masks, "level": lev, "x": cols(x).transpose(0, 2, 1),
        "s_ssd": s_ssd, "s_gdn": s_gdn.reshape(4, P, 2, 512),
        "w_ada": np.concatenate([blocks(w, KT_IN, 1) for w in f["w_ada"]]),
        "w_in0": blocks(sin, KT_IN, 1), "w_in1": blocks(gin, KT_IN, 1),
        "w_out0": blocks(f["ssd_w_out"][0], KT_IN, 2), "w_out1": blocks(f["gdn_w_out"][0], KT_IN, 2),
        "w_up0": up[0], "w_up1": up[1],
        "w_down0": blocks(f["ffn_w_down"][0], KT_DOWN, 2), "w_down1": blocks(f["ffn_w_down"][1], KT_DOWN, 2),
    }
    return {k: np.ascontiguousarray(a) for k, a in out.items()}


def kernel(**inputs):
    import numpy as np
    import concourse.bacc as bacc
    from concourse.bass_utils import run_bass_kernel_spmd as run

    nc = bacc.Bacc("TRN2", target_bir_lowering=False, num_devices=1)
    arrays, dram = {}, {}
    for name, a in layouts(inputs).items():
        arrays[name + "_in"] = a
        dram[name] = nc.dram_tensor(name + "_in", a.shape, F32, kind="ExternalInput").ap()
    for k in ("w_in", "w_out", "w_up", "w_down"):
        dram[k] = [dram.pop(k + "0"), dram.pop(k + "1")]
    for name, shape in (("y", (P, DT, TOK)), ("o_ssd", (SSD_G, P, 2, 256)), ("o_gdn", (4, P, 2, 512))):
        dram[name] = nc.dram_tensor(name + "_out", shape, F32, kind="ExternalOutput").ap()
    trunk(nc, dram)
    r = run(nc, [arrays], core_ids=[0]).results[0]
    y = r["y_out"].transpose(2, 1, 0).reshape(TOK, D)
    s = r["o_ssd_out"].transpose(2, 0, 3, 1).reshape(2, 1, 1, SSD_H, SSD_P, P)
    g = r["o_gdn_out"].reshape(4, P, 2, 4, P).transpose(2, 0, 3, 1, 4).reshape(2, 1, 1, GDN_H, P, P)
    got = (y[None, :P], y[None, P:], s[0], s[1], g[0], g[1])
    return tuple(np.ascontiguousarray(a) for a in got)
```
